# Optimizing a Trainium2 kernel written in Bass

```python
import math
import jax, jax.numpy as jnp
from jax import lax
import numpy as np

D_MODEL = 1024
BATCH = 1
SEQ = 512
DEPTH = 2

N_MIXERS = 2
HEAD_DIM = 64
N_HEADS = D_MODEL // HEAD_DIM
N_KV_HEADS = N_HEADS // 4
GROUP = N_HEADS // N_KV_HEADS
Q_DIM = N_HEADS * HEAD_DIM
KV_DIM = N_KV_HEADS * HEAD_DIM
QKV_DIM = Q_DIM + 2 * KV_DIM
WINDOW = 128
BLOCK = 128
ROT_DIM = HEAD_DIM // 4
ROPE_THETA = 500000.0
CONV_CH = D_MODEL
CONV_WIDTH = 31
D_FF = 2816
FFN_RES_WEIGHT = 0.5
NORM_EPS = 1e-6
LN_EPS = 1e-5
N_ATTN_LAYERS = (DEPTH + 1) // 2
N_CONV_LAYERS = DEPTH // 2

kernel_name = "hybrid_swa_sink_conformer_conv_macaron"

def rms_norm(x, g):
    xf = x.astype(jnp.float32)
    y = xf * lax.rsqrt(jnp.mean(xf * xf, axis=-1, keepdims=True) + NORM_EPS)
    return (y * g.astype(jnp.float32)).astype(x.dtype)

def layer_norm(x, g, b):
    xf = x.astype(jnp.float32)
    mu = jnp.mean(xf, axis=-1, keepdims=True)
    xc = xf - mu
    var = jnp.mean(xc * xc, axis=-1, keepdims=True)
    y = xc * lax.rsqrt(var + LN_EPS) * g.astype(jnp.float32) + b.astype(jnp.float32)
    return y.astype(x.dtype)

def swiglu(h, w_in, w_out):
    gu = h @ w_in
    gate, up = gu[..., :D_FF], gu[..., D_FF:]
    return (jax.nn.silu(gate) * up) @ w_out

def rope_tables(seq_len):
    pos = jnp.arange(seq_len, dtype=jnp.float32)
    inv_freq = ROPE_THETA ** (-jnp.arange(0, ROT_DIM, 2, dtype=jnp.float32) / ROT_DIM)
    ang = pos[:, None] * inv_freq[None, :]
    return jnp.cos(ang), jnp.sin(ang)

def apply_partial_rope(x, cos, sin):
    half = ROT_DIM // 2
    shape = (1, x.shape[1]) + (1,) * (x.ndim - 3) + (half,)
    c, s = cos.reshape(shape), sin.reshape(shape)
    xr = x[..., :ROT_DIM].astype(jnp.float32)
    x1, x2 = xr[..., :half], xr[..., half:]
    rot = jnp.concatenate([x1 * c - x2 * s, x2 * c + x1 * s], axis=-1).astype(x.dtype)
    return jnp.concatenate([rot, x[..., ROT_DIM:]], axis=-1)

def sliding_window_sink_attention(h, w_qkv, b_qkv, w_o, b_o, sinks, cos, sin):
    B, S, _ = h.shape
    nb = S // BLOCK
    qkv = h @ w_qkv + b_qkv
    q = qkv[..., :Q_DIM].reshape(B, S, N_KV_HEADS, GROUP, HEAD_DIM)
    k = qkv[..., Q_DIM:Q_DIM + KV_DIM].reshape(B, S, N_KV_HEADS, HEAD_DIM)
    v = qkv[..., Q_DIM + KV_DIM:].reshape(B, S, N_KV_HEADS, HEAD_DIM)
    q = apply_partial_rope(q, cos, sin)
    k = apply_partial_rope(k, cos, sin)

    qb = q.reshape(B, nb, BLOCK, N_KV_HEADS, GROUP, HEAD_DIM)
    kb = k.reshape(B, nb, BLOCK, N_KV_HEADS, HEAD_DIM)
    vb = v.reshape(B, nb, BLOCK, N_KV_HEADS, HEAD_DIM)
    k_prev = jnp.concatenate([jnp.zeros_like(kb[:, :1]), kb[:, :-1]], axis=1)
    v_prev = jnp.concatenate([jnp.zeros_like(vb[:, :1]), vb[:, :-1]], axis=1)
    kw = jnp.concatenate([k_prev, kb], axis=2)
    vw = jnp.concatenate([v_prev, vb], axis=2)

    scale = 1.0 / math.sqrt(HEAD_DIM)
    scores = jnp.einsum('bnqhgd,bnkhd->bnhgqk', qb, kw,
                        preferred_element_type=jnp.float32) * scale
    q_pos = jnp.arange(BLOCK)[:, None] + BLOCK
    k_pos = jnp.arange(2 * BLOCK)[None, :]
    diff = q_pos - k_pos
    band = (diff >= 0) & (diff < WINDOW)
    first = (jnp.arange(nb) == 0)[:, None, None] & (k_pos < BLOCK)[None]
    valid = band[None] & ~first
    scores = jnp.where(valid[None, :, None, None], scores, -1e30)
    sink = jnp.broadcast_to(
        sinks.astype(jnp.float32).reshape(1, 1, N_KV_HEADS, GROUP, 1, 1),
        scores.shape[:-1] + (1,))
    probs = jax.nn.softmax(jnp.concatenate([scores, sink], axis=-1), axis=-1)[..., :-1]
    out = jnp.einsum('bnhgqk,bnkhd->bnqhgd', probs.astype(vw.dtype), vw)
    out = out.reshape(B, S, Q_DIM)
    return out @ w_o + b_o

def conformer_conv_module(h, w_pw1, b_pw1, w_dw, b_dw, ln_g, ln_b, w_pw2, b_pw2):
    a = h @ w_pw1 + b_pw1
    u = a[..., :CONV_CH] * jax.nn.sigmoid(a[..., CONV_CH:])
    y = lax.conv_general_dilated(
        u, w_dw[:, None, :].astype(u.dtype), window_strides=(1,),
        padding=[(CONV_WIDTH - 1, 0)],
        dimension_numbers=('NWC', 'WIO', 'NWC'),
        feature_group_count=CONV_CH) + b_dw
    y = jax.nn.silu(layer_norm(y, ln_g, ln_b))
    return y @ w_pw2 + b_pw2

def setup_inputs(seed: int = 0) -> dict:
    key = jax.random.key(seed)
    ks = jax.random.split(key, 20)

    def nrm(k, shape, scale):
        return jax.random.normal(k, shape, jnp.float32) * scale

    na, nc = N_ATTN_LAYERS, N_CONV_LAYERS
    return {
        "x": nrm(ks[0], (BATCH, SEQ, D_MODEL), 1.0),
        "norm_pre": 1.0 + nrm(ks[1], (DEPTH, 3, D_MODEL), 0.05),
        "norm_post": 1.0 + nrm(ks[2], (DEPTH, 3, D_MODEL), 0.05),
        "w_ffn_in": nrm(ks[3], (DEPTH, 2, D_MODEL, 2 * D_FF), D_MODEL ** -0.5),
        "w_ffn_out": nrm(ks[4], (DEPTH, 2, D_FF, D_MODEL), D_FF ** -0.5),
        "attn_w_qkv": nrm(ks[5], (na, D_MODEL, QKV_DIM), D_MODEL ** -0.5),
        "attn_b_qkv": nrm(ks[6], (na, QKV_DIM), 0.02),
        "attn_w_o": nrm(ks[7], (na, Q_DIM, D_MODEL), Q_DIM ** -0.5),
        "attn_b_o": nrm(ks[8], (na, D_MODEL), 0.02),
        "attn_sinks": nrm(ks[9], (na, N_HEADS), 0.5),
        "conv_w_pw1": nrm(ks[10], (nc, D_MODEL, 2 * CONV_CH), D_MODEL ** -0.5),
        "conv_b_pw1": nrm(ks[11], (nc, 2 * CONV_CH), 0.02),
        "conv_w_dw": nrm(ks[12], (nc, CONV_WIDTH, CONV_CH), CONV_WIDTH ** -0.5),
        "conv_b_dw": nrm(ks[13], (nc, CONV_CH), 0.02),
        "conv_ln_g": 1.0 + nrm(ks[14], (nc, CONV_CH), 0.05),
        "conv_ln_b": nrm(ks[15], (nc, CONV_CH), 0.02),
        "conv_w_pw2": nrm(ks[16], (nc, CONV_CH, D_MODEL), CONV_CH ** -0.5),
        "conv_b_pw2": nrm(ks[17], (nc, D_MODEL), 0.02),
    }

def reference(x, norm_pre, norm_post, w_ffn_in, w_ffn_out,
              attn_w_qkv, attn_b_qkv, attn_w_o, attn_b_o, attn_sinks,
              conv_w_pw1, conv_b_pw1, conv_w_dw, conv_b_dw, conv_ln_g, conv_ln_b,
              conv_w_pw2, conv_b_pw2):
    h = x
    cos, sin = rope_tables(x.shape[1])
    for i in range(DEPTH):
        f = swiglu(rms_norm(h, norm_pre[i, 0]), w_ffn_in[i, 0], w_ffn_out[i, 0])
        h = h + FFN_RES_WEIGHT * rms_norm(f, norm_post[i, 0])
        t = rms_norm(h, norm_pre[i, 1])
        j = i // N_MIXERS
        if i % N_MIXERS == 0:
            t = sliding_window_sink_attention(t, attn_w_qkv[j], attn_b_qkv[j], attn_w_o[j],
                                              attn_b_o[j], attn_sinks[j], cos, sin)
        else:
            t = conformer_conv_module(t, conv_w_pw1[j], conv_b_pw1[j], conv_w_dw[j],
                                      conv_b_dw[j], conv_ln_g[j], conv_ln_b[j],
                                      conv_w_pw2[j], conv_b_pw2[j])
        h = h + rms_norm(t, norm_post[i, 1])
        f = swiglu(rms_norm(h, norm_pre[i, 2]), w_ffn_in[i, 1], w_ffn_out[i, 1])
        h = h + FFN_RES_WEIGHT * rms_norm(f, norm_post[i, 2])
    return h


_drawn_inputs = setup_inputs


def setup_inputs(seed=0):
    import zlib

    import numpy as np

    out = dict(_drawn_inputs(seed))
    spreads = {}
    factors = {'attn_sinks': 3.917, 'conv_b_pw1': 4.851, 'conv_ln_b': 5.182, 'conv_b_pw2': 3.273}
    for name, (base, spread) in spreads.items():
        noise = np.random.default_rng([zlib.crc32(name.encode()), seed]).standard_normal(out[name].shape)
        drawn = base * np.exp(spread * noise) if base else spread * noise
        out[name] = __import__('jax').numpy.asarray(drawn.astype(out[name].dtype))
    for name, factor in factors.items():
        out[name] = (out[name] * factor).astype(out[name].dtype)
    return out
```

```python
from contextlib import ExitStack

import numpy as np

import concourse.bass as bass
from concourse import mybir

F32 = mybir.dt.float32
F32R = mybir.dt.float32r
BF16 = mybir.dt.bfloat16
ALU = mybir.AluOpType
ACT = mybir.ActivationFunctionType
AX = mybir.AxisListType

P = 128
D = 1024
T = 512
KD = D // P
FF = 2816
KF = FF // P
FFN_GROUPS = (8, 8, 6)
HEADS, KV, HD = 16, 4, 64
GROUP = HEADS // KV
ROT, THETA = HD // 4, 500000.0
NB = T // P
CW = 31
RING = 4
BLK = 8
SLOT = BLK * P
EPS, LN_EPS = 1e-6, 1e-5
SUBS = 6
HALF_WEIGHT = (0, 2, 3, 5)

FFN_SLOTS = 2 * KF + KD * len(FFN_GROUPS)
QKV_SLOTS, DOWN_SLOTS, PW1_SLOTS = 12, KD, 2 * KD
FFN0 = 0
QKV = FFN0 + FFN_SLOTS
WO = QKV + QKV_SLOTS
FFN1 = WO + DOWN_SLOTS
FFN2 = FFN1 + FFN_SLOTS
PW1 = FFN2 + FFN_SLOTS
PW2 = PW1 + PW1_SLOTS
FFN3 = PW2 + DOWN_SLOTS
SLOTS = FFN3 + FFN_SLOTS

COLS, _at = {}, 0
for _name, _n in (("pre", SUBS * KD), ("post", SUBS * KD), ("b_qk", 10), ("b_o", KD), ("b_pw1", 2 * KD),
                  ("b_dw", KD), ("ln_g", KD), ("ln_b", KD), ("b_pw2", KD), ("w_dw", KD * CW),
                  ("sinks", HEADS), ("b_v", KV * HD)):
    COLS[_name] = _at
    _at += _n
N_COLS = _at


def head_of(cp, b, cc):
    c = 2 * cp + cc
    return (2 * (c // GROUP) + b) * GROUP + c % GROUP


def build_program(nc, stream, xT, cols_in, rope_c, rope_s, perm_in, ident_in, ident_b_in, mask_in, outT):
    ctx = ExitStack()
    with ctx:
        def sb(name, shape, dt=F32):
            return ctx.enter_context(nc.sbuf_tensor(name, shape, dt))

        def sem(name):
            return ctx.enter_context(nc.semaphore(name))

        h = sb("h_resid", [P, KD, T])
        x_hi, x_lo = sb("x_hi", [P, KD, T], F32R), sb("x_lo", [P, KD, T], F32R)
        a_hi, a_lo = sb("a_hi", [P, BLK, T], F32R), sb("a_lo", [P, BLK, T], F32R)
        f = sb("f_out", [P, KD, T])
        raw = sb("w_raw", [P, RING, SLOT])
        w_hi, w_lo = sb("w_hi", [P, RING, SLOT], F32R), sb("w_lo", [P, RING, SLOT], F32R)
        G, U = sb("gate_tmp", [P, 2, T]), sb("up_tmp", [P, 2, T])
        ss = sb("sum_sq", [P, T])
        sq = sb("sq_tmp", [P, 2, T])
        root = sb("root", [P, T])
        r_post, r_pre = sb("r_post", [P, T]), sb("r_pre", [P, T])
        cols = sb("cols", [P, N_COLS])
        rc, rs = sb("rope_cos", [P, T]), sb("rope_sin", [P, T])
        perm, ident = sb("rope_perm", [P, P]), sb("ident", [P, P])
        ident_b, mask = sb("ident_b", [P, P], BF16), sb("mask", [P, 2, 2 * 2 * P], BF16)
        ones = sb("ones", [P, P])
        eps, tiny = sb("eps", [P, 2]), sb("tiny", [P, 2])
        qT = sb("qT", [P, KD, T])
        kT = sb("kT", [P, 2, P + T])
        V = sb("V", [P, NB + 1, KV * HD])
        r_col, root_col = sb("r_col", [P, NB]), sb("root_col", [P, NB])
        mx, m_row, neg_m = sb("mx", [P, 2, 4]), sb("m_row", [P, 4]), sb("neg_m", [P, 2, 4])
        sink_in, sink_e = sb("sink_in", [P, 2, 4]), sb("sink_e", [P, 2, 4])
        row_sum, den = sb("row_sum", [P, 2, 4]), sb("den", [P, 4])
        fv = f[:, :, :].rearrange("p a n -> p (a n)")
        prob = [fv[:, i * 1024:(i + 1) * 1024].rearrange("p (j k) -> p j k", j=4) for i in range(2)]
        probT = [fv[:, 2048 + i * 1024:2048 + (i + 1) * 1024].rearrange("p (kb c) -> p kb c", kb=2)
                 for i in range(2)]
        Vf = V[:, :, :].rearrange("p a n -> p (a n)")
        PADT = CW - 1 + T
        u = [Vf[:, i * PADT:(i + 1) * PADT] for i in range(2)]
        y = qT

        bank = [ctx.enter_context(nc.psum_tensor(f"bank{i}", [P, T], F32)) for i in range(8)]
        STAT, AUX = bank[4], bank[5]

        s_raw = [sem(f"raw_loaded{i}") for i in range(RING)]
        s_h0 = [sem(f"x_loaded{k}") for k in range(KD)]
        s_const, s_cols = sem("consts_loaded"), sem("cols_loaded")
        s_memset = sem("memsets_done")
        s_hi, s_lo = sem("weight_hi"), sem("weight_lo")
        s_mm = sem("slot_multiplied")
        s_evac = sem("slot_evacuated")
        s_half = sem("post_gain_halved")
        s_xhi, s_x = sem("x_hi_ready"), sem("x_ready")
        s_hsq, s_hacc = sem("h_squared"), sem("h_sq_added")
        s_fsq, s_facc = sem("f_squared"), sem("f_sq_added")
        s_h = sem("h_updated")
        s_stat, s_root, s_rinv = sem("sum_sq_done"), sem("root_done"), sem("rms_inverted")
        s_act, s_prod, s_ahi, s_a = sem("gate_activated"), sem("gate_times_up"), sem("a_hi_ready"), sem("a_ready")
        s_dve = sem("vector_chain")
        s_qb, s_perm, s_rope = sem("qk_biased"), sem("qk_permuted"), sem("qk_rotated")
        s_cstat, s_croot, s_v = sem("col_stat"), sem("col_root"), sem("v_ready")
        s_qk, s_m, s_exp, s_p = sem("scores_ready"), sem("max_ready"), sem("exp_done"), sem("probs_ready")
        s_t, s_ta, s_tb = sem("probs_transposed"), sem("probT_prev"), sem("probT_own")
        s_pv, s_ohi, s_o = sem("pv_done"), sem("o_hi_ready"), sem("o_ready")
        s_u, s_y = sem("u_ready"), sem("y_ready")
        s_mu_mm, s_mu = sem("mean_summed"), sem("mean_ready")
        s_xc, s_lsq, s_lacc = sem("y_centred"), sem("y_squared"), sem("y_sq_added")
        s_lstat, s_lroot = sem("var_summed"), sem("var_root")
        s_z, s_zact, s_zhi, s_zlo = sem("z_ready"), sem("z_activated"), sem("z_hi_ready"), sem("z_ready_lo")
        s_out = sem("out_stored")

        def col(name, i):
            return cols[:, COLS[name] + i:COLS[name] + i + 1]

        def blk(ring, s, k, width=P):
            return ring[:, s, k * width:(k + 1) * width]

        block = ctx.enter_context(nc.Block())

        @block.sync
        def _(sp):
            for s in range(RING):
                sp.dma_start(raw[:, s, :], stream[s, :, :]).then_inc(s_raw[s], 16)
            with sp.Fori(1, SLOTS // RING) as i:
                for s in range(RING):
                    sp.wait_ge(s_lo, RING * i + (s - RING + 1))
                    sp.dma_start(raw[:, s, :], stream[bass.ds(RING * i + s, 1), :, :].rearrange("a p n -> p (a n)")
                                 ).then_inc(s_raw[s], 16)
            for m in range(KD):
                sp.wait_ge(s_h, (SUBS - 1) * KD + m + 1)
                sp.dma_start(outT[m * P:(m + 1) * P, :], h[:, m, :]).then_inc(s_out, 16)
            sp.wait_ge(s_out, 16 * KD)

        @block.gpsimd
        def _(pool):
            for dst, src in ((rc, rope_c), (rs, rope_s), (perm, perm_in), (ident, ident_in),
                             (ident_b, ident_b_in)):
                pool.dma_start(dst[:, :], src[:, :]).then_inc(s_const, 16)
            pool.dma_start(mask[:, :, :], mask_in[:, :, :]).then_inc(s_const, 16)
            nc.gpsimd.memset(kT[:, :, 0:P], 0.0).then_inc(s_memset, 1)
            nc.gpsimd.memset(V[:, 0, :], 0.0).then_inc(s_memset, 1)
            pool.wait_ge(s_pv, 4 * NB)
            for i in range(2):
                nc.gpsimd.memset(u[i][:, 0:CW - 1], 0.0).then_inc(s_memset, 1)

        CONSTS = 6 * 16

        @block.tensor
        def _(pe):
            def mm3(out, lw, lx, first, last):
                nc.tensor.matmul(out, lw[0], lx[0], start=first, stop=False)
                nc.tensor.matmul(out, lw[0], lx[1], start=False, stop=False)
                return nc.tensor.matmul(out, lw[1], lx[0], start=False, stop=last)

            def x_block(s, k, last=KD - 1):
                return mm3(bank[s][:, :], (blk(w_hi, s, k), blk(w_lo, s, k)), (x_hi[:, k, :], x_lo[:, k, :]),
                           k == 0, k == last)

            def sum_squares(out, part, rest):
                nc.tensor.matmul(out, ones[:, :], part, start=True, stop=False)
                return nc.tensor.matmul(out, ones[:, :], rest, start=False, stop=True)

            def first_body(n0, sub):
                for k in range(KD):
                    pe.wait_ge(s_x, KD * sub + k + 1)
                    if k == KD - 1:
                        pe.wait_ge(s_hacc, (KD - 2) * sub + KD - 2)
                        pe.wait_ge(s_hsq, KD * sub + KD)
                        pe.wait_ge(s_root, 2 * sub) if sub else None
                        sum_squares(STAT[:, :], f[:, 0, :], f[:, KD - 1, :]).then_inc(s_stat, 1)
                    for s in range(RING):
                        if k == 0:
                            pe.wait_ge(s_lo, n0 + s + 1)
                            if n0:
                                pe.wait_ge(s_evac, n0 + s - RING + 1)
                        last = x_block(s, k)
                        if k == KD - 1:
                            last.then_inc(s_mm, 1)

            def body(n, s):
                pe.wait_ge(s_lo, n + 1)
                pe.wait_ge(s_evac, n + (1 - RING))
                for k in range(KD):
                    last = x_block(s, k)
                last.then_inc(s_mm, 1)

            def bodies(n0, count):
                with pe.Fori(0, count // RING) as i:
                    for s in range(RING):
                        body(RING * i + (n0 + s), s)

            def down(n0, blocks, ready):
                with pe.Fori(0, KD // RING) as i:
                    for s in range(RING):
                        n = RING * i + (n0 + s)
                        pe.wait_ge(s_lo, n + 1)
                        pe.wait_ge(s_evac, n + (1 - RING))
                        for k in range(blocks):
                            if s == 0 and ready(k):
                                pe.wait_ge(*ready(k))
                            last = mm3(bank[s][:, :], (blk(w_hi, s, k), blk(w_lo, s, k)),
                                       (a_hi[:, k, :], a_lo[:, k, :]), k == 0, k == blocks - 1)
                        last.then_inc(s_mm, 1)

            def post_stat(sub):
                pe.wait_ge(s_facc, (KD - 2) * (sub + 1))
                pe.wait_ge(s_fsq, KD * (sub + 1))
                pe.wait_ge(s_root, 2 * sub + 1)
                sum_squares(STAT[:, :], ss[:, :], sq[:, 1, :]).then_inc(s_stat, 1)

            def ffn(n0, index, sub):
                n, q = n0, KF * index
                for g, chunks in enumerate(FFN_GROUPS):
                    if g == 0:
                        first_body(n, sub)
                        bodies(n + RING, 2 * chunks - RING)
                    else:
                        bodies(n, 2 * chunks)
                    n += 2 * chunks
                    down(n, chunks, lambda k, q=q: (s_a, q + k + 1))
                    n += KD
                    q += chunks
                post_stat(sub)

            def qkv(n0, sub):
                first_body(n0, sub)
                for t in range(NB):
                    for part, rest in ((f[:, 0, :], f[:, KD - 1, :]),):
                        nc.tensor.matmul(AUX[:, t:t + 1], part[:, t * P:(t + 1) * P], ones[:, 0:1],
                                         start=True, stop=False)
                        last = nc.tensor.matmul(AUX[:, t:t + 1], rest[:, t * P:(t + 1) * P], ones[:, 0:1],
                                                start=False, stop=True)
                last.then_inc(s_cstat, 1)
                pe.wait_ge(s_const, CONSTS)

                def permute(c):
                    pe.wait_ge(s_qb, c + 1)
                    if c >= 2:
                        pe.wait_ge(s_rope, c - 1)
                    src = kT[:, c, P:P + T] if c < 2 else qT[:, c - 2, :]
                    nc.tensor.matmul(bank[6 + c % 2][:, :], perm[:, :], src, start=True, stop=True
                                     ).then_inc(s_perm, 1)

                after = {4: (0, 1), 5: (2, 3), 6: (4, 5), 7: (6,), 8: (7,), 9: (8,)}
                for c in range(RING, 10):
                    body(n0 + c, c % RING)
                    for j in after[c]:
                        permute(j)
                for half in range(2):
                    n, s = n0 + 10 + half, 2 + half
                    pe.wait_ge(s_lo, n + 1)
                    if half == 0:
                        pe.wait_ge(s_evac, n0 + 10)
                    for t in range(NB):
                        for kk in range(4):
                            k = 4 * half + kk
                            w = blk(w_hi, s, kk, 2 * P), blk(w_lo, s, kk, 2 * P)
                            tok = slice(t * P, (t + 1) * P)
                            last = mm3(bank[t][:, 0:2 * P], (x_hi[:, k, tok], x_lo[:, k, tok]), w,
                                       k == 0, k == KD - 1)
                    last.then_inc(s_mm, 1)
                    if half == 0:
                        permute(9)

            def attention():
                def scores(t):
                    n, cp = divmod(t, 4)
                    if t == 0:
                        pe.wait_ge(s_rope, 10)
                        pe.wait_ge(s_memset, 3)
                        pe.wait_ge(s_evac, QKV + QKV_SLOTS)
                        pe.wait_ge(s_v, 2)
                    if t >= 2:
                        pe.wait_ge(s_exp, t - 1)
                    for b in range(2):
                        out = bank[(4, 0)[t % 2] + b]
                        nc.tensor.matmul(out[:, :], ident_b[:, :], mask[:, min(n, 1), :], start=True, stop=False)
                        for cc in range(2):
                            c, half = 2 * cp + cc, slice(b * HD, (b + 1) * HD)
                            last = nc.tensor.matmul(out[:, cc * 2 * P:(cc + 1) * 2 * P],
                                                    qT[half, c, n * P:(n + 1) * P],
                                                    kT[half, c // GROUP, n * P:(n + 2) * P],
                                                    start=False, stop=(cc == 1))
                    last.then_inc(s_qk, 1)

                def transposes(t):
                    pe.wait_ge(s_p, t + 1)
                    if t:
                        pe.wait_ge(s_ta, t)
                        pe.wait_ge(s_tb, t)
                    for kb in range(2):
                        for j in range(4):
                            last = nc.tensor.transpose(bank[6 + kb][:, j * P:(j + 1) * P],
                                                       prob[t % 2][:, j, kb * P:(kb + 1) * P], ident[:, :])
                    last.then_inc(s_t, 1)

                def values(t):
                    n, cp = divmod(t, 4)
                    kc = cp // 2
                    pe.wait_ge(s_ta, t + 1)
                    pe.wait_ge(s_tb, t + 1)
                    if t >= 2:
                        pe.wait_ge(s_o, t - 1)
                    for b in range(2):
                        for kb in range(2):
                            kv = 2 * kc + b
                            last = nc.tensor.matmul(bank[2 + t % 2][b * HD:(b + 1) * HD, 0:2 * P],
                                                    V[:, n + kb, kv * HD:(kv + 1) * HD],
                                                    probT[t % 2][:, kb, b * 2 * P:(b + 1) * 2 * P],
                                                    start=(kb == 0), stop=(kb == 1))
                    last.then_inc(s_pv, 1)

                steps = 4 * NB
                scores(0)
                for t in range(steps):
                    if t + 1 < steps:
                        scores(t + 1)
                    transposes(t)
                    if t:
                        values(t - 1)
                values(steps - 1)

            pe.wait_ge(s_memset, 1)
            ffn(FFN0, 0, 0)
            qkv(QKV, 1)
            attention()
            down(WO, KD, lambda k: (s_o, 4 * NB) if k == 0 else None)
            post_stat(1)
            ffn(FFN1, 1, 2)
            ffn(FFN2, 2, 3)
            first_body(PW1, 4)
            bodies(PW1 + RING, PW1_SLOTS - RING)
            pe.wait_ge(s_y, KD)
            nc.tensor.matmul(AUX[:, :], ones[:, :], ss[:, :], start=True, stop=True).then_inc(s_mu_mm, 1)
            pe.wait_ge(s_lacc, KD - 2)
            pe.wait_ge(s_lsq, KD)
            sum_squares(AUX[:, :], f[:, 0, :], f[:, KD - 1, :]).then_inc(s_lstat, 1)
            down(PW2, KD, lambda k: (s_zlo, k + 1))
            post_stat(4)
            ffn(FFN3, 3, 5)

        @block.scalar
        def _(act):
            def w_hi_of(n, s, turn, freed=True):
                act.wait_ge(s_raw[s], 16 * turn + 16)
                if freed:
                    act.wait_ge(s_mm, n + (1 - RING))
                nc.scalar.activation(w_hi[:, s, :], raw[:, s, :], ACT.Copy).then_inc(s_hi, 1)

            def next_slot(n, s, turn):
                w_hi_of(n + RING, s, turn + 1)

            def x_chunk(sub, k):
                nc.scalar.activation(x_hi[:, k, :], h[:, k, :], ACT.Copy, scale=col("pre", sub * KD + k)
                                     ).then_inc(s_xhi, 1)
                nc.scalar.activation(f[:, k, :], h[:, k, :], ACT.Square).then_inc(s_hsq, 1)

            def root_of(stat_count):
                act.wait_ge(s_stat, stat_count)
                if stat_count > 1:
                    act.wait_ge(s_rinv, stat_count - 1)
                nc.scalar.activation(root[:, :], STAT[:, :], ACT.Sqrt, bias=eps[:, 0:1], scale=1.0 / D
                                     ).then_inc(s_root, 1)

            def sqrt_table():
                nc.scalar.activation(tiny[:, 0:1], eps[:, 0:1], ACT.Sqrt)

            def pair_steps(n, s, turn, q, chunk):
                next_slot(n, s, turn)
                act.wait_ge(s_evac, n + 1)
                g = G[:, (s // 2) % 2, :]
                nc.scalar.activation(g, g, ACT.Silu).then_inc(s_act, 1)
                next_slot(n + 1, s + 1, turn)
                act.wait_ge(s_prod, q + 1)
                nc.scalar.activation(a_hi[:, chunk, :], U[:, (s // 2) % 2, :], ACT.Copy).then_inc(s_ahi, 1)

            def down(n0, last_of=None, stream_ends=False):
                if last_of is None:
                    with act.Fori(0, KD // RING) as i:
                        for s in range(RING):
                            next_slot(RING * i + (n0 + s), s, i + n0 // RING)
                    return
                for m in range(KD):
                    n, s = n0 + m, m % RING
                    more = n + RING < SLOTS
                    if more and m < KD - 1:
                        next_slot(n, s, n // RING)
                    if m == KD - 1:
                        sqrt_table()
                    act.wait_ge(s_evac, n + 1)
                    if m >= 3:
                        act.wait_ge(s_facc, (KD - 2) * last_of + m - 2)
                    nc.scalar.activation(ss[:, :] if m == 0 else sq[:, m % 2, :], f[:, m, :], ACT.Square
                                         ).then_inc(s_fsq, 1)
                    if more and m == KD - 1:
                        next_slot(n, s, n // RING)

            def boundary(sub):
                root_of(2 * sub + 2)
                if sub == SUBS - 1:
                    return
                for k in range(KD):
                    act.wait_ge(s_h, KD * sub + k + 1)
                    x_chunk(sub + 1, k)
                root_of(2 * sub + 3)

            def ffn(n0, index, sub):
                n, q = n0, KF * index
                for g, chunks in enumerate(FFN_GROUPS):
                    with act.Fori(0, 2 * chunks // RING) as i:
                        for p in range(2):
                            pair_steps(RING * i + (n + 2 * p), 2 * p, i + n // RING, 2 * i + (q + p),
                                       bass.ds(2 * i + p, 1))
                    n += 2 * chunks
                    down(n, sub if g == len(FFN_GROUPS) - 1 else None)
                    n += KD
                    q += chunks
                boundary(sub)

            def qkv(n0):
                act.wait_ge(s_cstat, 1)
                nc.scalar.activation(root_col[:, :], AUX[:, 0:NB], ACT.Sqrt, bias=eps[:, 0:1], scale=1.0 / D
                                     ).then_inc(s_croot, 1)
                for c in range(QKV_SLOTS):
                    n, s = n0 + c, c % RING
                    next_slot(n, s, n // RING)
                    if c < 10:
                        act.wait_ge(s_evac, n + 1)
                        dst = kT[:, c, P:P + T] if c < 2 else qT[:, c - 2, :]
                        nc.scalar.activation(dst, G[:, c % 2, :], ACT.Identity, bias=col("b_qk", c)
                                             ).then_inc(s_qb, 1)

            def attention():
                def exps(t):
                    act.wait_ge(s_m, t + 1)
                    if t >= 2:
                        act.wait_ge(s_t, t - 1)
                    for b in range(2):
                        for cc in range(2):
                            j = 2 * b + cc
                            nc.scalar.activation(prob[t % 2][:, j, :],
                                                 bank[(4, 0)[t % 2] + b][:, cc * 2 * P:(cc + 1) * 2 * P], ACT.Exp,
                                                 bias=neg_m[:, t % 2, j:j + 1], scale=HD ** -0.5,
                                                 accum_out=row_sum[:, t % 2, j:j + 1])
                    nc.scalar.activation(sink_e[:, t % 2, :], sink_in[:, t % 2, :], ACT.Exp).then_inc(s_exp, 1)

                def copy_prev(t):
                    act.wait_ge(s_t, t + 1)
                    if t >= 2:
                        act.wait_ge(s_pv, t - 1)
                    nc.scalar.activation(probT[t % 2][:, 0, :], bank[6][:, :], ACT.Copy).then_inc(s_ta, 1)

                def out_hi(t):
                    n, cp = divmod(t, 4)
                    act.wait_ge(s_pv, t + 1)
                    nc.scalar.activation(a_hi[:, 2 * cp:2 * cp + 2, n * P:(n + 1) * P],
                                         bank[2 + t % 2][:, 0:2 * P].rearrange("p (c q) -> p c q", c=2), ACT.Copy
                                         ).then_inc(s_ohi, 1)

                steps = 4 * NB
                exps(0)
                for t in range(steps):
                    if t + 1 < steps:
                        exps(t + 1)
                    copy_prev(t)
                    if t:
                        out_hi(t - 1)
                out_hi(steps - 1)

            def conv(n0):
                for j in range(KD):
                    for e in range(2):
                        n = n0 + 2 * j + e
                        s = n % RING
                        next_slot(n, s, n // RING)
                        if e == 1:
                            act.wait_ge(s_evac, n + 1)
                            g = G[:, j % 2, :]
                            nc.scalar.activation(g, g, ACT.Sigmoid, bias=col("b_pw1", KD + j)).then_inc(s_act, 1)
                act.wait_ge(s_mu_mm, 1)
                nc.scalar.activation(r_post[:, :], AUX[:, :], ACT.Copy, scale=1.0 / D).then_inc(s_mu, 1)
                sqrt_table()
                for m in range(KD):
                    act.wait_ge(s_xc, m + 1)
                    nc.scalar.activation(f[:, m, :], y[:, m, :], ACT.Square).then_inc(s_lsq, 1)
                act.wait_ge(s_lstat, 1)
                nc.scalar.activation(root[:, :], AUX[:, :], ACT.Sqrt, bias=eps[:, 1:2], scale=1.0 / D
                                     ).then_inc(s_lroot, 1)
                nc.scalar.activation(tiny[:, 1:2], eps[:, 0:1], ACT.Silu)
                for m in range(KD):
                    act.wait_ge(s_z, m + 1)
                    nc.scalar.activation(y[:, m, :], y[:, m, :], ACT.Silu, bias=col("ln_b", m),
                                         scale=col("ln_g", m)).then_inc(s_zact, 1)
                    act.wait_ge(s_zact, m + 1)
                    nc.scalar.activation(a_hi[:, m, :], y[:, m, :], ACT.Copy).then_inc(s_zhi, 1)

            act.dma_start(cols[:, :], cols_in[:, :]).then_inc(s_cols, 16)
            for k in range(KD):
                act.dma_start(h[:, k, :], xT[k * P:(k + 1) * P, :]).then_inc(s_h0[k], 16)
            act.wait_ge(s_half, 1)
            sqrt_table()
            for s in range(RING):
                w_hi_of(s, s, 0, freed=False)
            for k in range(KD):
                act.wait_ge(s_h0[k], 16)
                x_chunk(0, k)
            root_of(1)
            ffn(FFN0, 0, 0)
            qkv(QKV)
            attention()
            down(WO, 1)
            boundary(1)
            ffn(FFN1, 1, 2)
            ffn(FFN2, 2, 3)
            conv(PW1)
            down(PW2, 4)
            boundary(4)
            ffn(FFN3, 3, 5)

        @block.vector
        def _(dve):
            chain = [0]

            def link(ins):
                chain[0] += 1
                ins.then_inc(s_dve, 1)
                dve.wait_ge(s_dve, chain[0])

            def w_lo_of(n, s):
                dve.wait_ge(s_hi, n + 1)
                nc.vector.tensor_tensor(w_lo[:, s, :], raw[:, s, :], w_hi[:, s, :].bitcast(F32), ALU.subtract
                                        ).then_inc(s_lo, 1)

            def next_slot(n, s):
                w_lo_of(n + RING, s)

            def invert(dst, count):
                dve.wait_ge(s_root, count)
                nc.vector.reciprocal(dst[:, :], root[:, :]).then_inc(s_rinv, 1)
                dve.wait_ge(s_rinv, count)

            def x_lo_of(sub, k):
                dve.wait_ge(s_xhi, KD * sub + k + 1)
                nc.vector.scalar_tensor_tensor(out=x_lo[:, k, :], in0=h[:, k, :], scalar=col("pre", sub * KD + k),
                                               in1=x_hi[:, k, :].bitcast(F32), op0=ALU.mult, op1=ALU.subtract
                                               ).then_inc(s_x, 1)

            def add_h_square(sub, k):
                dve.wait_ge(s_hsq, KD * sub + k + 1)
                if k > 1:
                    dve.wait_ge(s_hacc, (KD - 2) * sub + k - 1)
                nc.vector.tensor_tensor(f[:, 0, :], f[:, 0, :], f[:, k, :], ALU.add).then_inc(s_hacc, 1)

            def scale_to(dst, s, n):
                dve.wait_ge(s_mm, n + 1)
                nc.vector.tensor_tensor(dst, bank[s][:, :], r_pre[:, :], ALU.mult).then_inc(s_evac, 1)

            def pair_steps(n, s, q, chunk):
                p = (s // 2) % 2
                next_slot(n, s)
                scale_to(G[:, p, :], s, n)
                next_slot(n + 1, s + 1)
                scale_to(U[:, p, :], s + 1, n + 1)
                dve.wait_ge(s_evac, n + 2)
                dve.wait_ge(s_act, q + 1)
                nc.vector.tensor_tensor(U[:, p, :], U[:, p, :], G[:, p, :], ALU.mult).then_inc(s_prod, 1)
                dve.wait_ge(s_ahi, q + 1)
                nc.vector.tensor_tensor(a_lo[:, chunk, :], U[:, p, :], a_hi[:, chunk, :].bitcast(F32), ALU.subtract
                                        ).then_inc(s_a, 1)

            def evacuate(n, s, m, how):
                dve.wait_ge(s_mm, n + 1)
                if how == "set":
                    ins = nc.vector.tensor_copy(f[:, m, :], bank[s][:, :])
                elif how == "add":
                    ins = nc.vector.tensor_tensor(f[:, m, :], bank[s][:, :], f[:, m, :], ALU.add)
                else:
                    ins = nc.vector.tensor_scalar(f[:, m, :], bank[s][:, :], col(how, m), None, ALU.add)
                ins.then_inc(s_evac, 1)

            def add_f_square(sub, m):
                dve.wait_ge(s_fsq, KD * sub + m + 1)
                if m > 1:
                    dve.wait_ge(s_facc, (KD - 2) * sub + m - 1)
                nc.vector.tensor_tensor(ss[:, :], ss[:, :], sq[:, m % 2, :], ALU.add).then_inc(s_facc, 1)

            def down(n0, how, last_of=None):
                if last_of is None:
                    with dve.Fori(0, KD // RING) as i:
                        for s in range(RING):
                            n = RING * i + (n0 + s)
                            next_slot(n, s)
                            evacuate(n, s, bass.ds(RING * i + s, 1), how)
                    return
                for m in range(KD):
                    n, s = n0 + m, m % RING
                    more = n + RING < SLOTS
                    if more and m < KD - 1:
                        next_slot(n, s)
                    evacuate(n, s, m, how)
                    if m >= 2:
                        add_f_square(last_of, m - 1)
                    if more and m == KD - 1:
                        next_slot(n, s)

            def boundary(sub):
                invert(r_post, 2 * sub + 2)

                def normalise(k):
                    nc.vector.tensor_tensor(f[:, k, :], f[:, k, :], r_post[:, :], ALU.mult).then_inc(s_dve, 1)
                    chain[0] += 1

                def add_residual(k):
                    dve.wait_ge(s_dve, chain[0])
                    nc.vector.scalar_tensor_tensor(out=h[:, k, :], in0=f[:, k, :], scalar=col("post", sub * KD + k),
                                                   in1=h[:, k, :], op0=ALU.mult, op1=ALU.add).then_inc(s_h, 1)

                last = sub == SUBS - 1
                for k in range(KD):
                    normalise(k)
                    if k and not last:
                        x_lo_of(sub + 1, k - 1)
                    add_residual(k)
                    if k >= 2 and not last:
                        add_h_square(sub + 1, k - 1)
                if not last:
                    x_lo_of(sub + 1, KD - 1)
                    invert(r_pre, 2 * sub + 3)

            def ffn(n0, index, sub):
                n, q = n0, KF * index
                for g, chunks in enumerate(FFN_GROUPS):
                    with dve.Fori(0, 2 * chunks // RING) as i:
                        for p in range(2):
                            pair_steps(RING * i + (n + 2 * p), 2 * p, 2 * i + (q + p), bass.ds(2 * i + p, 1))
                    n += 2 * chunks
                    down(n, "add" if g else "set", sub if g == len(FFN_GROUPS) - 1 else None)
                    n += KD
                    q += chunks
                boundary(sub)

            def qkv(n0):
                dve.wait_ge(s_croot, 1)
                link(nc.vector.reciprocal(r_col[:, :], root_col[:, :]))
                dve.wait_ge(s_const, CONSTS)

                def rotate(c):
                    x = kT[:, c, P:P + T] if c < 2 else qT[:, c - 2, :]
                    dve.wait_ge(s_perm, c + 1)
                    nc.vector.tensor_tensor(U[:, 0, :], bank[6 + c % 2][:, :], rs[:, :], ALU.mult)
                    link(nc.vector.tensor_tensor(U[:, 1, :], x, rc[:, :], ALU.mult))
                    nc.vector.tensor_tensor(x, U[:, 0, :], U[:, 1, :], ALU.add).then_inc(s_rope, 1)
                    dve.wait_ge(s_rope, c + 1)

                after = {4: (0, 1), 5: (2, 3), 6: (4, 5), 7: (6,), 8: (7,), 9: (8,), 10: (9,)}
                for c in range(QKV_SLOTS):
                    n, s = n0 + c, c % RING
                    next_slot(n, s)
                    if c < 10:
                        if c >= 2:
                            dve.wait_ge(s_qb, c - 1)
                        scale_to(G[:, c % 2, :], s, n)
                    for j in after.get(c, ()):
                        rotate(j)
                dve.wait_ge(s_mm, n0 + QKV_SLOTS)
                for t in range(NB):
                    nc.vector.scalar_tensor_tensor(out=V[:, t + 1, :], in0=bank[t][:, 0:2 * P],
                                                   scalar=r_col[:, t:t + 1],
                                                   in1=cols[:, COLS["b_v"]:COLS["b_v"] + 2 * P],
                                                   op0=ALU.mult, op1=ALU.add).then_inc(s_evac if t < 2 else s_v, 1)

            def attention():
                def maxima(t):
                    n, cp = divmod(t, 4)
                    i = t % 2
                    sinks = cols[:, COLS["sinks"] + 4 * cp:COLS["sinks"] + 4 * cp + 4]
                    dve.wait_ge(s_qk, t + 1)
                    if t >= 2:
                        dve.wait_ge(s_exp, t - 1)
                    for b in range(2):
                        ins = nc.vector.reduce_max(mx[:, i, 2 * b:2 * b + 2],
                                                   bank[(4, 0)[i] + b][:, :].rearrange("p (c k) -> p c k", c=2),
                                                   axis=AX.X)
                    link(ins)
                    link(nc.vector.scalar_tensor_tensor(out=m_row[:, :], in0=mx[:, i, :], scalar=HD ** -0.5,
                                                        in1=sinks, op0=ALU.mult, op1=ALU.max))
                    nc.vector.tensor_scalar(neg_m[:, i, :], m_row[:, :], -1.0, None, ALU.mult)
                    nc.vector.tensor_tensor(sink_in[:, i, :], sinks, m_row[:, :], ALU.subtract).then_inc(s_m, 1)

                def normalise(t):
                    i = t % 2
                    dve.wait_ge(s_exp, t + 1)
                    link(nc.vector.tensor_tensor(den[:, :], row_sum[:, i, :], sink_e[:, i, :], ALU.add))
                    link(nc.vector.reciprocal(den[:, :], den[:, :]))
                    for j in range(4):
                        ins = nc.vector.tensor_scalar(prob[i][:, j, :], prob[i][:, j, :], den[:, j:j + 1], None,
                                                      ALU.mult)
                    ins.then_inc(s_p, 1)

                def copy_own(t):
                    dve.wait_ge(s_t, t + 1)
                    if t >= 2:
                        dve.wait_ge(s_pv, t - 1)
                    nc.vector.tensor_copy(probT[t % 2][:, 1, :], bank[7][:, :]).then_inc(s_tb, 1)

                def out_lo(t):
                    n, cp = divmod(t, 4)
                    at = slice(2 * cp, 2 * cp + 2), slice(n * P, (n + 1) * P)
                    dve.wait_ge(s_ohi, t + 1)
                    nc.vector.tensor_tensor(a_lo[:, at[0], at[1]],
                                            bank[2 + t % 2][:, 0:2 * P].rearrange("p (c q) -> p c q", c=2),
                                            a_hi[:, at[0], at[1]].bitcast(F32), ALU.subtract).then_inc(s_o, 1)

                steps = 4 * NB
                maxima(0)
                for t in range(steps):
                    if t + 1 < steps:
                        maxima(t + 1)
                    normalise(t)
                    copy_own(t)
                    if t:
                        out_lo(t - 1)
                out_lo(steps - 1)

            def conv(n0, acts):
                for j in range(KD):
                    p = j % 2
                    for e in range(2):
                        n = n0 + 2 * j + e
                        next_slot(n, n % RING)
                        scale_to((U, G)[e][:, p, :], n % RING, n)
                    if j == 0:
                        dve.wait_ge(s_memset, 5)
                    dve.wait_ge(s_act, acts + j + 1)
                    link(nc.vector.scalar_tensor_tensor(out=u[p][:, CW - 1:], in0=U[:, p, :],
                                                        scalar=col("b_pw1", j), in1=G[:, p, :],
                                                        op0=ALU.add, op1=ALU.mult))
                    link(nc.vector.tensor_scalar(y[:, j, :], u[p][:, 0:T], col("w_dw", j * CW), col("b_dw", j),
                                                 ALU.mult, ALU.add))
                    for w in range(1, CW):
                        link(nc.vector.scalar_tensor_tensor(out=y[:, j, :], in0=u[p][:, w:w + T],
                                                            scalar=col("w_dw", j * CW + w), in1=y[:, j, :],
                                                            op0=ALU.mult, op1=ALU.add))
                    if j == 0:
                        ins = nc.vector.tensor_copy(ss[:, :], y[:, 0, :])
                    else:
                        dve.wait_ge(s_y, j)
                        ins = nc.vector.tensor_tensor(ss[:, :], ss[:, :], y[:, j, :], ALU.add)
                    ins.then_inc(s_y, 1)
                dve.wait_ge(s_mu, 1)
                for m in range(KD):
                    nc.vector.tensor_tensor(y[:, m, :], y[:, m, :], r_post[:, :], ALU.subtract).then_inc(s_xc, 1)
                    if m >= 2:
                        add_y_square(m - 1)
                dve.wait_ge(s_lroot, 1)
                link(nc.vector.reciprocal(root[:, :], root[:, :]))
                for m in range(KD):
                    nc.vector.tensor_tensor(y[:, m, :], y[:, m, :], root[:, :], ALU.mult).then_inc(s_z, 1)
                    if m:
                        z_lo_of(m - 1)
                z_lo_of(KD - 1)

            def add_y_square(m):
                dve.wait_ge(s_lsq, m + 1)
                if m > 1:
                    dve.wait_ge(s_lacc, m - 1)
                nc.vector.tensor_tensor(f[:, 0, :], f[:, 0, :], f[:, m, :], ALU.add).then_inc(s_lacc, 1)

            def z_lo_of(m):
                dve.wait_ge(s_zhi, m + 1)
                nc.vector.tensor_tensor(a_lo[:, m, :], y[:, m, :], a_hi[:, m, :].bitcast(F32), ALU.subtract
                                        ).then_inc(s_zlo, 1)

            nc.vector.memset(ones[:, :], 1.0).then_inc(s_memset, 1)
            nc.vector.memset(eps[:, 0:1], EPS)
            link(nc.vector.memset(eps[:, 1:2], LN_EPS))
            dve.wait_ge(s_cols, 16)
            for sub in HALF_WEIGHT:
                at = cols[:, COLS["post"] + sub * KD:COLS["post"] + (sub + 1) * KD]
                ins = nc.vector.tensor_scalar(at, at, 0.5, None, ALU.mult)
            ins.then_inc(s_half, 1)
            dve.wait_ge(s_half, 1)
            for s in range(RING):
                w_lo_of(s, s)
            for k in range(KD):
                x_lo_of(0, k)
                if 1 <= k <= KD - 2:
                    add_h_square(0, k)
            invert(r_pre, 1)
            ffn(FFN0, 0, 0)
            qkv(QKV)
            attention()
            down(WO, "b_o", 1)
            boundary(1)
            ffn(FFN1, 1, 2)
            ffn(FFN2, 2, 3)
            conv(PW1, 3 * KF)
            down(PW2, "b_pw2", 4)
            boundary(4)
            ffn(FFN3, 3, 5)


def up_slots(w):
    n = w.shape[1] // P
    return w.reshape(KD, P, n, P).transpose(2, 1, 0, 3).reshape(n, P, SLOT)


def down_slots(w):
    k = w.shape[0] // P
    out = np.zeros((KD, P, BLK, P), w.dtype)
    out[:, :, :k] = w.reshape(k, P, KD, P).transpose(2, 1, 0, 3)
    return out.reshape(KD, P, SLOT)


def ffn_slots(w_in, w_out):
    pairs = np.stack([up_slots(w_in[:, :FF]), up_slots(w_in[:, FF:])], 1)
    parts, c = [], 0
    for chunks in FFN_GROUPS:
        parts.append(pairs[c:c + chunks].reshape(2 * chunks, P, SLOT))
        parts.append(down_slots(w_out[c * P:(c + chunks) * P]))
        c += chunks
    return parts


def tables():
    pos = np.arange(T, dtype=np.float32)
    inv = np.float32(THETA) ** (-np.arange(0, ROT, 2, dtype=np.float32) / np.float32(ROT))
    ang = pos[None, :] * inv.astype(np.float32)[:, None]
    rc, rs = np.ones((P, T), np.float32), np.zeros((P, T), np.float32)
    perm = np.zeros((P, P), np.float32)
    r = ROT // 2
    for o in range(0, P, HD):
        rc[o:o + r] = rc[o + r:o + ROT] = np.cos(ang)
        rs[o:o + r], rs[o + r:o + ROT] = -np.sin(ang), np.sin(ang)
        for i in range(r):
            perm[o + i, o + r + i] = perm[o + r + i, o + i] = 1.0
    q, k = np.arange(P)[:, None], np.arange(2 * P)[None, :]
    diff = q + P - k
    band = (diff >= 0) & (diff < P)
    mask = np.zeros((P, 2, 2, 2 * P), np.float32)
    mask[:, 0] = np.where(band & (k >= P), 0.0, -1e30)[:, None]
    mask[:, 1] = np.where(band, 0.0, -1e30)[:, None]
    return rc, rs, perm, np.eye(P, dtype=np.float32), mask.reshape(P, 2, 4 * P)


def kernel(x, norm_pre, norm_post, w_ffn_in, w_ffn_out, attn_w_qkv, attn_b_qkv, attn_w_o, attn_b_o, attn_sinks,
           conv_w_pw1, conv_b_pw1, conv_w_dw, conv_b_dw, conv_ln_g, conv_ln_b, conv_w_pw2, conv_b_pw2):
    import concourse.bacc as bacc
    import ml_dtypes
    from concourse.bass_utils import run_bass_kernel_spmd

    given = dict(locals())
    (x, norm_pre, norm_post, w_ffn_in, w_ffn_out, w_qkv, b_qkv, w_o, b_o, sinks, w_pw1, b_pw1, w_dw, b_dw, ln_g, ln_b,
     w_pw2, b_pw2) = (np.asarray(given[n]) for n in kernel.__code__.co_varnames[:kernel.__code__.co_argcount])

    heads = [head_of(c // 2, b, c % 2) for c in range(KD) for b in range(2)]
    q_cols = np.concatenate([np.arange(hd * HD, (hd + 1) * HD) for hd in heads])
    q_dim, kv_dim = HEADS * HD, KV * HD
    qk_cols = np.concatenate([q_dim + np.arange(kv_dim), q_cols])
    w_v = w_qkv[0][:, q_dim + kv_dim:].reshape(2, 4, P, kv_dim).transpose(0, 2, 1, 3).reshape(2, P, SLOT)
    pw1 = np.stack([up_slots(w_pw1[0][:, :D]), up_slots(w_pw1[0][:, D:])], 1).reshape(2 * KD, P, SLOT)
    stream = np.concatenate(
        ffn_slots(w_ffn_in[0, 0], w_ffn_out[0, 0])
        + [up_slots(w_qkv[0][:, qk_cols]), w_v, down_slots(w_o[0][q_cols])]
        + ffn_slots(w_ffn_in[0, 1], w_ffn_out[0, 1]) + ffn_slots(w_ffn_in[1, 0], w_ffn_out[1, 0])
        + [pw1, down_slots(w_pw2[0])] + ffn_slots(w_ffn_in[1, 1], w_ffn_out[1, 1]))

    def cols(v):
        return v.reshape(-1, P).T

    sink_order = [head_of(cp, b, cc) for cp in range(4) for b in range(2) for cc in range(2)]
    col_in = np.concatenate(
        [cols(norm_pre), cols(norm_post), cols(b_qkv[0][qk_cols]), cols(b_o), cols(b_pw1), cols(b_dw), cols(ln_g),
         cols(ln_b), cols(b_pw2), w_dw[0].reshape(CW, KD, P).transpose(2, 1, 0).reshape(P, KD * CW),
         np.broadcast_to(sinks[0][sink_order], (P, HEADS)), np.broadcast_to(b_qkv[0][q_dim + kv_dim:], (P, kv_dim))], 1)
    rc, rs, perm, ident, mask = tables()
    bf = ml_dtypes.bfloat16
    ins = {"stream": stream, "xT": np.ascontiguousarray(x[0].T), "cols_in": np.ascontiguousarray(col_in),
           "rope_c": rc, "rope_s": rs, "perm_in": perm, "ident_in": ident, "ident_b_in": ident.astype(bf),
           "mask_in": mask.astype(bf)}

    nc = bacc.Bacc("TRN2", target_bir_lowering=False, num_devices=1)
    args = [nc.dram_tensor(n, a.shape, mybir.dt.from_np(a.dtype), kind="ExternalInput").ap() for n, a in ins.items()]
    out = nc.dram_tensor("outT", (D, T), F32, kind="ExternalOutput").ap()
    build_program(nc, *args, out)
    r = run_bass_kernel_spmd(nc, [ins], core_ids=[0])
    return np.ascontiguousarray(r.results[0]["outT"].T)[None]
```

```python
from contextlib import ExitStack

import numpy as np

import concourse.bass as bass
from concourse import mybir

F32 = mybir.dt.float32
F32R = mybir.dt.float32r
BF16 = mybir.dt.bfloat16
ALU = mybir.AluOpType
ACT = mybir.ActivationFunctionType
AX = mybir.AxisListType

P = 128
D = 1024
T = 512
KD = D // P
FF = 2816
KF = FF // P
FFN_GROUPS = (8, 8, 6)
HEADS, KV, HD = 16, 4, 64
GROUP = HEADS // KV
ROT, THETA = HD // 4, 500000.0
NB = T // P
CW = 31
RING = 4
BLK = 8
SLOT = BLK * P
EPS, LN_EPS = 1e-6, 1e-5
PE_TAPS = 12
SUBS = 6
HALF_WEIGHT = (0, 2, 3, 5)

FFN_SLOTS = 2 * KF + KD * len(FFN_GROUPS)
QKV_SLOTS, DOWN_SLOTS, PW1_SLOTS = 12, KD, 2 * KD
FFN0 = 0
QKV = FFN0 + FFN_SLOTS
WO = QKV + QKV_SLOTS
FFN1 = WO + DOWN_SLOTS
FFN2 = FFN1 + FFN_SLOTS
PW1 = FFN2 + FFN_SLOTS
PW2 = PW1 + PW1_SLOTS
FFN3 = PW2 + DOWN_SLOTS
SLOTS = FFN3 + FFN_SLOTS

COLS, _at = {}, 0
for _name, _n in (("pre", SUBS * KD), ("post", SUBS * KD), ("b_qk", 10), ("b_o", KD), ("b_pw1", 2 * KD),
                  ("b_dw", KD), ("ln_g", KD), ("ln_b", KD), ("b_pw2", KD), ("w_dw", KD * CW),
                  ("sinks", HEADS), ("b_v", KV * HD)):
    COLS[_name] = _at
    _at += _n
N_COLS = _at


def head_of(cp, b, cc):
    c = 2 * cp + cc
    return (2 * (c // GROUP) + b) * GROUP + c % GROUP


def build_program(nc, stream, xT, cols_in, rope_c, rope_s, perm_in, ident_in, ident_b_in, mask_in, outT):
    ctx = ExitStack()
    with ctx:
        def sb(name, shape, dt=F32):
            return ctx.enter_context(nc.sbuf_tensor(name, shape, dt))

        def sem(name):
            return ctx.enter_context(nc.semaphore(name))

        h = sb("h_resid", [P, KD, T])
        x_hi, x_lo = sb("x_hi", [P, KD, T], F32R), sb("x_lo", [P, KD, T], F32R)
        a_hi, a_lo = sb("a_hi", [P, BLK, T], F32R), sb("a_lo", [P, BLK, T], F32R)
        f = sb("f_out", [P, KD, T])
        raw = sb("w_raw", [P, RING, SLOT])
        w_hi, w_lo = sb("w_hi", [P, RING, SLOT], F32R), sb("w_lo", [P, RING, SLOT], F32R)
        G, U = sb("gate_tmp", [P, 2, T]), sb("up_tmp", [P, 2, T])
        ss = sb("sum_sq", [P, T])
        sq = sb("sq_tmp", [P, 2, T])
        diag = sb("diag", [P, NB, P])
        r_pre = sb("r_pre", [P, T])
        mean = sb("mean", [P, T])
        cols = sb("cols", [P, N_COLS])
        rc, rs = sb("rope_cos", [P, T]), sb("rope_sin", [P, T])
        perm, ident = sb("rope_perm", [P, P]), sb("ident", [P, P])
        ident_b, mask = sb("ident_b", [P, P], BF16), sb("mask", [P, 2, 2 * 2 * P], BF16)
        ones = sb("ones", [P, P])
        eps, tiny = sb("eps", [P, 2]), sb("tiny", [P, 2])
        qT = sb("qT", [P, KD, T])
        kT = sb("kT", [P, 2, P + T])
        V = sb("V", [P, NB + 1, KV * HD])
        r_col, root_col = sb("r_col", [P, NB]), sb("root_col", [P, NB])
        dw_hi, dw_lo = sb("dw_hi", [P, KD * CW], F32R), sb("dw_lo", [P, KD * CW])
        mx, m_row, neg_m = sb("mx", [P, 2, 4]), sb("m_row", [P, 4]), sb("neg_m", [P, 2, 4])
        sink_in, sink_e = sb("sink_in", [P, 2, 4]), sb("sink_e", [P, 2, 4])
        row_sum, den = sb("row_sum", [P, 2, 4]), sb("den", [P, 4])
        fv = f[:, :, :].rearrange("p a n -> p (a n)")
        prob = [fv[:, i * 1024:(i + 1) * 1024].rearrange("p (j k) -> p j k", j=4) for i in range(2)]
        probT = [fv[:, 2048 + i * 1024:2048 + (i + 1) * 1024].rearrange("p (kb c) -> p kb c", kb=2)
                 for i in range(2)]
        Vf = V[:, :, :].rearrange("p a n -> p (a n)")
        PADT = CW - 1 + T
        u = [Vf[:, i * PADT:(i + 1) * PADT] for i in range(2)]
        y = qT
        def conv_views(a):
            flat = a[:, :, :].rearrange("p a n -> p (a n)")
            d = flat[:, PADT + 2:PADT + 2 + 2 * PE_TAPS * P].rearrange("p (i w c) -> p i w c", i=2, w=PE_TAPS)
            return flat[:, 0:PADT], d

        (u_hi, tap_hi), (u_lo, tap_lo) = conv_views(a_hi), conv_views(a_lo)

        bank = [ctx.enter_context(nc.psum_tensor(f"bank{i}", [P, T], F32)) for i in range(8)]
        STAT, BCAST = bank[4], bank[5]

        s_raw = [sem(f"raw_loaded{i}") for i in range(RING)]
        s_h0 = [sem(f"x_loaded{k}") for k in range(KD)]
        s_const, s_cols = sem("consts_loaded"), sem("cols_loaded")
        s_memset = sem("memsets_done")
        s_hi, s_lo = sem("weight_hi"), sem("weight_lo")
        s_mm = sem("slot_multiplied")
        s_evac = sem("slot_evacuated")
        s_half = sem("post_gain_halved")
        s_xhi, s_x = sem("x_hi_ready"), sem("x_ready")
        s_hsq, s_hacc = sem("h_squared"), sem("h_sq_added")
        s_fsq, s_facc = sem("f_squared"), sem("f_sq_added")
        s_h = sem("h_updated")
        s_stat, s_root, s_diag = sem("sum_sq_done"), sem("root_done"), sem("rms_inverted")
        s_bc, s_rpre = sem("rms_broadcast"), sem("r_pre_ready")
        s_act, s_prod, s_ahi, s_a = sem("gate_activated"), sem("gate_times_up"), sem("a_hi_ready"), sem("a_ready")
        s_dve = sem("vector_chain")
        s_qb, s_perm, s_rope = sem("qk_biased"), sem("qk_permuted"), sem("qk_rotated")
        s_v = sem("v_ready")
        s_qk, s_m, s_exp, s_p = sem("scores_ready"), sem("max_ready"), sem("exp_done"), sem("probs_ready")
        s_t, s_ta, s_tb = sem("probs_transposed"), sem("probT_prev"), sem("probT_own")
        s_pv, s_ohi, s_o = sem("pv_done"), sem("o_hi_ready"), sem("o_ready")
        s_sig, s_u, s_y = sem("gate_sigmoid"), sem("u_ready"), sem("y_ready")
        s_mu_mm, s_mu = sem("mean_summed"), sem("mean_ready")
        s_xc, s_lsq = sem("y_centred"), sem("y_squared")
        s_lstat, s_lroot, s_ldiag, s_lbc = sem("var_summed"), sem("var_root"), sem("std_inverted"), sem("std_broadcast")
        s_dwhi, s_dw = sem("dw_hi_ready"), sem("dw_ready")
        s_uhi, s_ulo, s_tap, s_cv = sem("u_hi_ready"), sem("u_lo_ready"), sem("taps_ready"), sem("pe_taps_done")
        s_z, s_zact, s_zhi, s_zlo = sem("z_ready"), sem("z_activated"), sem("z_hi_ready"), sem("z_ready_lo")
        s_out = sem("out_stored")

        def col(name, i):
            return cols[:, COLS[name] + i:COLS[name] + i + 1]

        def blk(ring, s, k, width=P):
            return ring[:, s, k * width:(k + 1) * width]

        block = ctx.enter_context(nc.Block())

        @block.sync
        def _(sp):
            for s in range(RING):
                sp.dma_start(raw[:, s, :], stream[s, :, :]).then_inc(s_raw[s], 16)
            with sp.Fori(1, SLOTS // RING) as i:
                for s in range(RING):
                    sp.wait_ge(s_lo, RING * i + (s - RING + 1))
                    sp.dma_start(raw[:, s, :], stream[bass.ds(RING * i + s, 1), :, :].rearrange("a p n -> p (a n)")
                                 ).then_inc(s_raw[s], 16)
            for m in range(KD):
                sp.wait_ge(s_h, (SUBS - 1) * KD + m + 1)
                sp.dma_start(outT[m * P:(m + 1) * P, :], h[:, m, :]).then_inc(s_out, 16)
            sp.wait_ge(s_out, 16 * KD)

        @block.gpsimd
        def _(pool):
            for dst, src in ((rc, rope_c), (rs, rope_s), (perm, perm_in), (ident, ident_in),
                             (ident_b, ident_b_in)):
                pool.dma_start(dst[:, :], src[:, :]).then_inc(s_const, 16)
            pool.dma_start(mask[:, :, :], mask_in[:, :, :]).then_inc(s_const, 16)
            nc.gpsimd.memset(kT[:, :, 0:P], 0.0).then_inc(s_memset, 1)
            nc.gpsimd.memset(V[:, 0, :], 0.0).then_inc(s_memset, 1)
            pool.wait_ge(s_pv, 4 * NB)
            for i in range(2):
                nc.gpsimd.memset(u[i][:, 0:CW - 1], 0.0).then_inc(s_memset, 1)

        CONSTS = 6 * 16

        @block.tensor
        def _(pe):
            def mm3(out, lw, lx, first, last):
                nc.tensor.matmul(out, lw[0], lx[0], start=first, stop=False)
                nc.tensor.matmul(out, lw[0], lx[1], start=False, stop=False)
                return nc.tensor.matmul(out, lw[1], lx[0], start=False, stop=last)

            def x_block(s, k, last=KD - 1):
                return mm3(bank[s][:, :], (blk(w_hi, s, k), blk(w_lo, s, k)), (x_hi[:, k, :], x_lo[:, k, :]),
                           k == 0, k == last)

            def add_columns(src, first, last):
                for t in range(NB):
                    ins = nc.tensor.matmul(STAT[:, t:t + 1], src[:, t * P:(t + 1) * P], ones[:, 0:1],
                                           start=(first and t == 0), stop=last, skip_group_check=True)
                return ins

            def broadcast():
                return nc.tensor.matmul(BCAST[:, :], ones[:, :], diag[:, :, :].rearrange("p t c -> p (t c)"),
                                        start=True, stop=True)

            def four_slots(n0, blocks, hi_ready, lo_ready, before_last, among_last):
                x = {KD: (x_hi, x_lo), -KD: (a_hi, a_lo)}[blocks]
                for k in range(KD):
                    if k == KD - 1:
                        before_last()
                    pe.wait_ge(*hi_ready(k))
                    for s in range(RING):
                        if k == 0:
                            pe.wait_ge(s_lo, n0 + s + 1)
                            if n0:
                                pe.wait_ge(s_evac, n0 + s - RING + 1)
                        nc.tensor.matmul(bank[s][:, :], blk(w_hi, s, k), x[0][:, k, :], start=(k == 0), stop=False)
                        nc.tensor.matmul(bank[s][:, :], blk(w_lo, s, k), x[0][:, k, :], start=False, stop=False)
                    pe.wait_ge(*lo_ready(k))
                    for s in range(RING):
                        if k == KD - 1 and s == 2:
                            among_last()
                        last = nc.tensor.matmul(bank[s][:, :], blk(w_hi, s, k), x[1][:, k, :], start=False,
                                                stop=(k == KD - 1))
                        if k == KD - 1:
                            last.then_inc(s_mm, 1)

            def first_body(n0, sub):
                def columns():
                    if sub:
                        pe.wait_ge(s_root, 2 * sub)
                    pe.wait_ge(s_hacc, (KD - 2) * sub + KD - 2)
                    add_columns(f[:, 0, :], True, False)
                    pe.wait_ge(s_hsq, KD * sub + KD)
                    add_columns(f[:, KD - 1, :], False, True).then_inc(s_stat, 1)

                def spread():
                    pe.wait_ge(s_diag, 2 * sub + 1)
                    if sub:
                        pe.wait_ge(s_h, KD * sub)
                    broadcast().then_inc(s_bc, 1)

                four_slots(n0, KD, lambda k: (s_xhi, KD * sub + k + 1), lambda k: (s_x, KD * sub + k + 1),
                           columns, spread)

            def body(n, s):
                pe.wait_ge(s_lo, n + 1)
                pe.wait_ge(s_evac, n + (1 - RING))
                for k in range(KD):
                    last = x_block(s, k)
                last.then_inc(s_mm, 1)

            def bodies(n0, count):
                with pe.Fori(0, count // RING) as i:
                    for s in range(RING):
                        body(RING * i + (n0 + s), s)

            def down(n0, blocks, ready):
                with pe.Fori(0, KD // RING) as i:
                    for s in range(RING):
                        n = RING * i + (n0 + s)
                        pe.wait_ge(s_lo, n + 1)
                        pe.wait_ge(s_evac, n + (1 - RING))
                        for k in range(blocks):
                            if s == 0 and ready(k):
                                pe.wait_ge(*ready(k))
                            last = mm3(bank[s][:, :], (blk(w_hi, s, k), blk(w_lo, s, k)),
                                       (a_hi[:, k, :], a_lo[:, k, :]), k == 0, k == blocks - 1)
                        last.then_inc(s_mm, 1)

            def post_stat(sub):
                pe.wait_ge(s_root, 2 * sub + 1)
                pe.wait_ge(s_facc, (KD - 2) * (sub + 1))
                add_columns(ss, True, False)
                pe.wait_ge(s_fsq, KD * (sub + 1))
                add_columns(sq[:, 1, :], False, True).then_inc(s_stat, 1)
                pe.wait_ge(s_diag, 2 * sub + 2)
                pe.wait_ge(s_rpre, sub + 1)
                broadcast().then_inc(s_bc, 1)

            def ffn(n0, index, sub):
                n, q = n0, KF * index
                for g, chunks in enumerate(FFN_GROUPS):
                    if g == 0:
                        first_body(n, sub)
                        bodies(n + RING, 2 * chunks - RING)
                    else:
                        bodies(n, 2 * chunks)
                    n += 2 * chunks
                    down(n, chunks, lambda k, q=q: (s_a, q + k + 1))
                    n += KD
                    q += chunks
                post_stat(sub)

            def qkv(n0, sub):
                first_body(n0, sub)
                pe.wait_ge(s_const, CONSTS)

                def permute(c):
                    pe.wait_ge(s_qb, c + 1)
                    if c >= 2:
                        pe.wait_ge(s_rope, c - 1)
                    src = kT[:, c, P:P + T] if c < 2 else qT[:, c - 2, :]
                    nc.tensor.matmul(bank[6 + c % 2][:, :], perm[:, :], src, start=True, stop=True
                                     ).then_inc(s_perm, 1)

                after = {4: (0, 1), 5: (2, 3), 6: (4, 5), 7: (6,), 8: (7,), 9: (8,)}
                for c in range(RING, 10):
                    body(n0 + c, c % RING)
                    for j in after[c]:
                        permute(j)
                for half in range(2):
                    n, s = n0 + 10 + half, 2 + half
                    pe.wait_ge(s_lo, n + 1)
                    if half == 0:
                        pe.wait_ge(s_evac, n0 + 10)
                    for t in range(NB):
                        for kk in range(4):
                            k = 4 * half + kk
                            w = blk(w_hi, s, kk, 2 * P), blk(w_lo, s, kk, 2 * P)
                            tok = slice(t * P, (t + 1) * P)
                            last = mm3(bank[t][:, 0:2 * P], (x_hi[:, k, tok], x_lo[:, k, tok]), w,
                                       k == 0, k == KD - 1)
                    last.then_inc(s_mm, 1)
                    if half == 0:
                        permute(9)

            def attention():
                def scores(t):
                    n, cp = divmod(t, 4)
                    if t == 0:
                        pe.wait_ge(s_rope, 10)
                        pe.wait_ge(s_memset, 3)
                        pe.wait_ge(s_evac, QKV + QKV_SLOTS)
                        pe.wait_ge(s_v, 2)
                        pe.wait_ge(s_rpre, 2)
                    if t >= 2:
                        pe.wait_ge(s_exp, t - 1)
                    for b in range(2):
                        out = bank[(4, 0)[t % 2] + b]
                        nc.tensor.matmul(out[:, :], ident_b[:, :], mask[:, min(n, 1), :], start=True, stop=False)
                        for cc in range(2):
                            c, half = 2 * cp + cc, slice(b * HD, (b + 1) * HD)
                            last = nc.tensor.matmul(out[:, cc * 2 * P:(cc + 1) * 2 * P],
                                                    qT[half, c, n * P:(n + 1) * P],
                                                    kT[half, c // GROUP, n * P:(n + 2) * P],
                                                    start=False, stop=(cc == 1))
                    last.then_inc(s_qk, 1)

                def transposes(t):
                    pe.wait_ge(s_p, t + 1)
                    if t:
                        pe.wait_ge(s_ta, t)
                        pe.wait_ge(s_tb, t)
                    for kb in range(2):
                        for j in range(4):
                            last = nc.tensor.transpose(bank[6 + kb][:, j * P:(j + 1) * P],
                                                       prob[t % 2][:, j, kb * P:(kb + 1) * P], ident[:, :])
                    last.then_inc(s_t, 1)

                def values(t):
                    n, cp = divmod(t, 4)
                    kc = cp // 2
                    pe.wait_ge(s_ta, t + 1)
                    pe.wait_ge(s_tb, t + 1)
                    if t >= 2:
                        pe.wait_ge(s_o, t - 1)
                    for b in range(2):
                        for kb in range(2):
                            kv = 2 * kc + b
                            last = nc.tensor.matmul(bank[2 + t % 2][b * HD:(b + 1) * HD, 0:2 * P],
                                                    V[:, n + kb, kv * HD:(kv + 1) * HD],
                                                    probT[t % 2][:, kb, b * 2 * P:(b + 1) * 2 * P],
                                                    start=(kb == 0), stop=(kb == 1))
                    last.then_inc(s_pv, 1)

                steps = 4 * NB
                scores(0)
                scores(1)
                for t in range(steps):
                    transposes(t)
                    if t:
                        values(t - 1)
                    if t + 2 < steps:
                        scores(t + 2)
                values(steps - 1)

            def convolution(n0, sub):
                def taps(j):
                    out = bank[6 + j % 2][:, :]
                    pe.wait_ge(s_uhi, j + 1)
                    pe.wait_ge(s_ulo, j + 1)
                    pe.wait_ge(s_tap, j + 1)
                    if j >= 2:
                        pe.wait_ge(s_y, j - 1)
                    for w in range(PE_TAPS):
                        last = mm3(out, (tap_hi[:, j % 2, w, :], tap_lo[:, j % 2, w, :]),
                                   (u_hi[:, w:w + T], u_lo[:, w:w + T]), w == 0, w == PE_TAPS - 1)
                    last.then_inc(s_cv, 1)

                first_body(n0, sub)
                taps(0)
                for j in range(2, KD):
                    body(n0 + 2 * j, 2 * j % RING)
                    body(n0 + 2 * j + 1, (2 * j + 1) % RING)
                    taps(j - 1)
                taps(KD - 1)

            def layer_norm():
                pe.wait_ge(s_y, KD)
                nc.tensor.matmul(BCAST[:, :], ones[:, :], ss[:, :], start=True, stop=True).then_inc(s_mu_mm, 1)
                for m in range(KD):
                    pe.wait_ge(s_lsq, m + 1)
                    last = add_columns(f[:, m, :], m == 0, m == KD - 1)
                last.then_inc(s_lstat, 1)
                pe.wait_ge(s_ldiag, 1)
                pe.wait_ge(s_mu, 1)
                broadcast().then_inc(s_lbc, 1)
                four_slots(PW2, -KD, lambda k: (s_zhi, k + 1), lambda k: (s_zlo, k + 1),
                           lambda: None, lambda: None)
                for s in range(RING):
                    n = PW2 + RING + s
                    pe.wait_ge(s_lo, n + 1)
                    pe.wait_ge(s_evac, n - RING + 1)
                    for k in range(KD):
                        last = mm3(bank[s][:, :], (blk(w_hi, s, k), blk(w_lo, s, k)),
                                   (a_hi[:, k, :], a_lo[:, k, :]), k == 0, k == KD - 1)
                    last.then_inc(s_mm, 1)

            pe.wait_ge(s_memset, 1)
            ffn(FFN0, 0, 0)
            qkv(QKV, 1)
            attention()
            down(WO, KD, lambda k: (s_o, 4 * (NB - 1) + k // 2 + 1))
            post_stat(1)
            ffn(FFN1, 1, 2)
            ffn(FFN2, 2, 3)
            convolution(PW1, 4)
            layer_norm()
            post_stat(4)
            ffn(FFN3, 3, 5)

        @block.scalar
        def _(act):
            def w_hi_of(n, s, turn, freed=True):
                act.wait_ge(s_raw[s], 16 * turn + 16)
                if freed:
                    act.wait_ge(s_mm, n + (1 - RING))
                nc.scalar.activation(w_hi[:, s, :], raw[:, s, :], ACT.Copy).then_inc(s_hi, 1)

            def next_slot(n, s, turn):
                w_hi_of(n + RING, s, turn + 1)

            def x_chunk(sub, k):
                nc.scalar.activation(x_hi[:, k, :], h[:, k, :], ACT.Copy, scale=col("pre", sub * KD + k)
                                     ).then_inc(s_xhi, 1)
                nc.scalar.activation(f[:, k, :], h[:, k, :], ACT.Square).then_inc(s_hsq, 1)

            def root_of(stat_count):
                act.wait_ge(s_stat, stat_count)
                if stat_count > 1:
                    act.wait_ge(s_diag, stat_count - 1)
                nc.scalar.activation(root_col[:, :], STAT[:, 0:NB], ACT.Sqrt, bias=eps[:, 0:1], scale=1.0 / D
                                     ).then_inc(s_root, 1)

            def keep_r_pre(sub):
                act.wait_ge(s_bc, 2 * sub + 1)
                nc.scalar.activation(r_pre[:, :], BCAST[:, :], ACT.Copy).then_inc(s_rpre, 1)

            def sqrt_table():
                nc.scalar.activation(tiny[:, 0:1], eps[:, 0:1], ACT.Sqrt)

            def pair_steps(n, s, turn, q, chunk):
                next_slot(n, s, turn)
                act.wait_ge(s_evac, n + 1)
                g = G[:, (s // 2) % 2, :]
                nc.scalar.activation(g, g, ACT.Silu).then_inc(s_act, 1)
                act.wait_ge(s_prod, q + 1)
                nc.scalar.activation(a_hi[:, chunk, :], U[:, (s // 2) % 2, :], ACT.Copy).then_inc(s_ahi, 1)
                next_slot(n + 1, s + 1, turn)

            def down(n0, last_of=None, stream_ends=False):
                if last_of is None:
                    with act.Fori(0, KD // RING) as i:
                        for s in range(RING):
                            next_slot(RING * i + (n0 + s), s, i + n0 // RING)
                    return
                for m in range(KD):
                    n, s = n0 + m, m % RING
                    more = n + RING < SLOTS
                    if more and m < KD - 1:
                        next_slot(n, s, n // RING)
                    if m == KD - 1:
                        sqrt_table()
                    act.wait_ge(s_evac, n + 1)
                    if m >= 3:
                        act.wait_ge(s_facc, (KD - 2) * last_of + m - 2)
                    nc.scalar.activation(ss[:, :] if m == 0 else sq[:, m % 2, :], f[:, m, :], ACT.Square
                                         ).then_inc(s_fsq, 1)
                    if more and m == KD - 1:
                        next_slot(n, s, n // RING)

            def boundary(sub):
                root_of(2 * sub + 2)
                if sub == SUBS - 1:
                    return
                for k in range(KD):
                    act.wait_ge(s_h, KD * sub + k + 1)
                    x_chunk(sub + 1, k)
                root_of(2 * sub + 3)
                keep_r_pre(sub + 1)

            def ffn(n0, index, sub):
                n, q = n0, KF * index
                for g, chunks in enumerate(FFN_GROUPS):
                    with act.Fori(0, 2 * chunks // RING) as i:
                        for p in range(2):
                            pair_steps(RING * i + (n + 2 * p), 2 * p, i + n // RING, 2 * i + (q + p),
                                       bass.ds(2 * i + p, 1))
                    n += 2 * chunks
                    down(n, sub if g == len(FFN_GROUPS) - 1 else None)
                    n += KD
                    q += chunks
                boundary(sub)

            def qkv(n0):
                for c in range(QKV_SLOTS):
                    n, s = n0 + c, c % RING
                    next_slot(n, s, n // RING)
                    if c < 10:
                        act.wait_ge(s_evac, n + 1)
                        dst = kT[:, c, P:P + T] if c < 2 else qT[:, c - 2, :]
                        nc.scalar.activation(dst, G[:, c % 2, :], ACT.Identity, bias=col("b_qk", c)
                                             ).then_inc(s_qb, 1)

            def attention():
                def exps(t):
                    act.wait_ge(s_m, t + 1)
                    if t >= 2:
                        act.wait_ge(s_t, t - 1)
                    for b in range(2):
                        for cc in range(2):
                            j = 2 * b + cc
                            nc.scalar.activation(prob[t % 2][:, j, :],
                                                 bank[(4, 0)[t % 2] + b][:, cc * 2 * P:(cc + 1) * 2 * P], ACT.Exp,
                                                 bias=neg_m[:, t % 2, j:j + 1], scale=HD ** -0.5,
                                                 accum_out=row_sum[:, t % 2, j:j + 1])
                    nc.scalar.activation(sink_e[:, t % 2, :], sink_in[:, t % 2, :], ACT.Exp).then_inc(s_exp, 1)

                def copy_prev(t):
                    act.wait_ge(s_t, t + 1)
                    if t >= 2:
                        act.wait_ge(s_pv, t - 1)
                    nc.scalar.activation(probT[t % 2][:, 0, :], bank[6][:, :], ACT.Copy).then_inc(s_ta, 1)

                def out_hi(t):
                    n, cp = divmod(t, 4)
                    act.wait_ge(s_pv, t + 1)
                    nc.scalar.activation(a_hi[:, 2 * cp:2 * cp + 2, n * P:(n + 1) * P],
                                         bank[2 + t % 2][:, 0:2 * P].rearrange("p (c q) -> p c q", c=2), ACT.Copy
                                         ).then_inc(s_ohi, 1)

                steps = 4 * NB
                exps(0)
                for t in range(steps):
                    if t + 1 < steps:
                        exps(t + 1)
                    copy_prev(t)
                    if t:
                        out_hi(t - 1)
                out_hi(steps - 1)

            def conv(n0):
                def diagonals(j):
                    if j >= 2:
                        act.wait_ge(s_cv, j - 1)
                    for w in range(PE_TAPS):
                        at = slice(j * CW + w, j * CW + w + 1)
                        nc.scalar.activation(tap_hi[:, j % 2, w, :], ident[:, :], ACT.Copy,
                                             scale=dw_hi[:, at].bitcast(F32))
                        ins = nc.scalar.activation(tap_lo[:, j % 2, w, :], ident[:, :], ACT.Copy, scale=dw_lo[:, at])
                    ins.then_inc(s_tap, 1)

                act.wait_ge(s_const, CONSTS)
                act.wait_ge(s_dw, 1)
                diagonals(0)
                for j in range(KD):
                    for e in range(2):
                        n = n0 + 2 * j + e
                        s = n % RING
                        next_slot(n, s, n // RING)
                    act.wait_ge(s_evac, n + 1)
                    g = G[:, j % 2, :]
                    nc.scalar.activation(g, g, ACT.Sigmoid, bias=col("b_pw1", KD + j)).then_inc(s_sig, 1)
                    act.wait_ge(s_u, j + 1)
                    if j:
                        act.wait_ge(s_cv, j)
                    nc.scalar.activation(u_hi, u[j % 2], ACT.Copy).then_inc(s_uhi, 1)
                    if j + 1 < KD:
                        diagonals(j + 1)
                act.wait_ge(s_mu_mm, 1)
                nc.scalar.activation(mean[:, :], BCAST[:, :], ACT.Copy, scale=1.0 / D).then_inc(s_mu, 1)
                sqrt_table()
                for m in range(KD):
                    act.wait_ge(s_xc, m + 1)
                    nc.scalar.activation(f[:, m, :], y[:, m, :], ACT.Square).then_inc(s_lsq, 1)
                act.wait_ge(s_lstat, 1)
                nc.scalar.activation(root_col[:, :], STAT[:, 0:NB], ACT.Sqrt, bias=eps[:, 1:2], scale=1.0 / D
                                     ).then_inc(s_lroot, 1)
                nc.scalar.activation(tiny[:, 1:2], eps[:, 0:1], ACT.Silu)
                for m in range(KD):
                    act.wait_ge(s_z, m + 1)
                    nc.scalar.activation(y[:, m, :], y[:, m, :], ACT.Silu, bias=col("ln_b", m),
                                         scale=col("ln_g", m)).then_inc(s_zact, 1)
                    act.wait_ge(s_zact, m + 1)
                    nc.scalar.activation(a_hi[:, m, :], y[:, m, :], ACT.Copy).then_inc(s_zhi, 1)

            act.dma_start(cols[:, :], cols_in[:, :]).then_inc(s_cols, 16)
            for k in range(KD):
                act.dma_start(h[:, k, :], xT[k * P:(k + 1) * P, :]).then_inc(s_h0[k], 16)
            act.wait_ge(s_half, 1)
            sqrt_table()
            for s in range(RING):
                w_hi_of(s, s, 0, freed=False)
            nc.scalar.activation(dw_hi[:, :], cols[:, COLS["w_dw"]:COLS["w_dw"] + KD * CW], ACT.Copy
                                 ).then_inc(s_dwhi, 1)
            for k in range(KD):
                act.wait_ge(s_h0[k], 16)
                x_chunk(0, k)
            root_of(1)
            keep_r_pre(0)
            ffn(FFN0, 0, 0)
            qkv(QKV)
            attention()
            down(WO, 1)
            boundary(1)
            ffn(FFN1, 1, 2)
            ffn(FFN2, 2, 3)
            conv(PW1)
            down(PW2, 4)
            boundary(4)
            ffn(FFN3, 3, 5)

        @block.vector
        def _(dve):
            chain = [0]

            def link(ins):
                chain[0] += 1
                ins.then_inc(s_dve, 1)
                dve.wait_ge(s_dve, chain[0])

            def w_lo_of(n, s):
                dve.wait_ge(s_hi, n + 1)
                nc.vector.tensor_tensor(w_lo[:, s, :], raw[:, s, :], w_hi[:, s, :].bitcast(F32), ALU.subtract
                                        ).then_inc(s_lo, 1)

            def next_slot(n, s):
                w_lo_of(n + RING, s)

            def on_diagonals(done):
                link(nc.vector.reciprocal(r_col[:, :], root_col[:, :]))
                nc.vector.tensor_tensor(diag[:, :, :], ident[:, None, :].broadcast_to([P, NB, P]),
                                        r_col[:, :, None].broadcast_to([P, NB, P]), ALU.mult).then_inc(done, 1)

            def invert(count):
                dve.wait_ge(s_root, count)
                if count > 1:
                    dve.wait_ge(s_bc, count - 1)
                on_diagonals(s_diag)

            def x_lo_of(sub, k):
                dve.wait_ge(s_xhi, KD * sub + k + 1)
                nc.vector.scalar_tensor_tensor(out=x_lo[:, k, :], in0=h[:, k, :], scalar=col("pre", sub * KD + k),
                                               in1=x_hi[:, k, :].bitcast(F32), op0=ALU.mult, op1=ALU.subtract
                                               ).then_inc(s_x, 1)

            def add_h_square(sub, k):
                dve.wait_ge(s_hsq, KD * sub + k + 1)
                if k > 1:
                    dve.wait_ge(s_hacc, (KD - 2) * sub + k - 1)
                nc.vector.tensor_tensor(f[:, 0, :], f[:, 0, :], f[:, k, :], ALU.add).then_inc(s_hacc, 1)

            def scale_to(dst, s, n, rpre=None):
                dve.wait_ge(s_mm, n + 1)
                if rpre:
                    dve.wait_ge(s_rpre, rpre)
                nc.vector.tensor_tensor(dst, bank[s][:, :], r_pre[:, :], ALU.mult).then_inc(s_evac, 1)

            def pair_steps(n, s, q, chunk, rpre):
                p = (s // 2) % 2
                next_slot(n, s)
                scale_to(G[:, p, :], s, n, rpre)
                scale_to(U[:, p, :], s + 1, n + 1)
                dve.wait_ge(s_evac, n + 2)
                dve.wait_ge(s_act, q + 1)
                nc.vector.tensor_tensor(U[:, p, :], U[:, p, :], G[:, p, :], ALU.mult).then_inc(s_prod, 1)
                dve.wait_ge(s_ahi, q + 1)
                nc.vector.tensor_tensor(a_lo[:, chunk, :], U[:, p, :], a_hi[:, chunk, :].bitcast(F32), ALU.subtract
                                        ).then_inc(s_a, 1)
                next_slot(n + 1, s + 1)

            def evacuate(n, s, m, how):
                dve.wait_ge(s_mm, n + 1)
                if how == "set":
                    ins = nc.vector.tensor_copy(f[:, m, :], bank[s][:, :])
                elif how == "add":
                    ins = nc.vector.tensor_tensor(f[:, m, :], bank[s][:, :], f[:, m, :], ALU.add)
                else:
                    ins = nc.vector.tensor_scalar(f[:, m, :], bank[s][:, :], col(how, m), None, ALU.add)
                ins.then_inc(s_evac, 1)

            def add_f_square(sub, m):
                dve.wait_ge(s_fsq, KD * sub + m + 1)
                if m > 1:
                    dve.wait_ge(s_facc, (KD - 2) * sub + m - 1)
                nc.vector.tensor_tensor(ss[:, :], ss[:, :], sq[:, m % 2, :], ALU.add).then_inc(s_facc, 1)

            def down(n0, how, last_of=None):
                if last_of is None:
                    with dve.Fori(0, KD // RING) as i:
                        for s in range(RING):
                            n = RING * i + (n0 + s)
                            next_slot(n, s)
                            evacuate(n, s, bass.ds(RING * i + s, 1), how)
                    return
                for m in range(KD):
                    n, s = n0 + m, m % RING
                    more = n + RING < SLOTS
                    if more and m < KD - 1:
                        next_slot(n, s)
                    evacuate(n, s, m, how)
                    if m >= 2:
                        add_f_square(last_of, m - 1)
                    if more and m == KD - 1:
                        next_slot(n, s)

            def boundary(sub):
                invert(2 * sub + 2)
                dve.wait_ge(s_bc, 2 * sub + 2)

                def normalise(k):
                    nc.vector.tensor_tensor(f[:, k, :], f[:, k, :], BCAST[:, :], ALU.mult).then_inc(s_dve, 1)
                    chain[0] += 1

                def add_residual(k):
                    dve.wait_ge(s_dve, chain[0])
                    nc.vector.scalar_tensor_tensor(out=h[:, k, :], in0=f[:, k, :], scalar=col("post", sub * KD + k),
                                                   in1=h[:, k, :], op0=ALU.mult, op1=ALU.add).then_inc(s_h, 1)

                last = sub == SUBS - 1
                for k in range(KD):
                    normalise(k)
                    if k and not last:
                        x_lo_of(sub + 1, k - 1)
                    add_residual(k)
                    if k >= 2 and not last:
                        add_h_square(sub + 1, k - 1)
                if not last:
                    x_lo_of(sub + 1, KD - 1)
                    invert(2 * sub + 3)

            def ffn(n0, index, sub):
                n, q = n0, KF * index
                for g, chunks in enumerate(FFN_GROUPS):
                    with dve.Fori(0, 2 * chunks // RING) as i:
                        for p in range(2):
                            pair_steps(RING * i + (n + 2 * p), 2 * p, 2 * i + (q + p), bass.ds(2 * i + p, 1),
                                       sub + 1)
                    n += 2 * chunks
                    down(n, "add" if g else "set", sub if g == len(FFN_GROUPS) - 1 else None)
                    n += KD
                    q += chunks
                boundary(sub)

            def qkv(n0):
                dve.wait_ge(s_const, CONSTS)

                def rotate(c):
                    x = kT[:, c, P:P + T] if c < 2 else qT[:, c - 2, :]
                    dve.wait_ge(s_perm, c + 1)
                    nc.vector.tensor_tensor(U[:, 0, :], bank[6 + c % 2][:, :], rs[:, :], ALU.mult)
                    link(nc.vector.tensor_tensor(U[:, 1, :], x, rc[:, :], ALU.mult))
                    nc.vector.tensor_tensor(x, U[:, 0, :], U[:, 1, :], ALU.add).then_inc(s_rope, 1)
                    dve.wait_ge(s_rope, c + 1)

                after = {4: (0, 1), 5: (2, 3), 6: (4, 5), 7: (6,), 8: (7,), 9: (8,), 10: (9,)}
                for c in range(QKV_SLOTS):
                    n, s = n0 + c, c % RING
                    next_slot(n, s)
                    if c < 10:
                        if c >= 2:
                            dve.wait_ge(s_qb, c - 1)
                        scale_to(G[:, c % 2, :], s, n, 2)
                    for j in after.get(c, ()):
                        rotate(j)
                dve.wait_ge(s_mm, n0 + QKV_SLOTS)
                for t in range(NB):
                    nc.vector.scalar_tensor_tensor(out=V[:, t + 1, :], in0=bank[t][:, 0:2 * P],
                                                   scalar=r_col[:, t:t + 1],
                                                   in1=cols[:, COLS["b_v"]:COLS["b_v"] + 2 * P],
                                                   op0=ALU.mult, op1=ALU.add).then_inc(s_evac if t < 2 else s_v, 1)

            def attention():
                def maxima(t):
                    n, cp = divmod(t, 4)
                    i = t % 2
                    sinks = cols[:, COLS["sinks"] + 4 * cp:COLS["sinks"] + 4 * cp + 4]
                    dve.wait_ge(s_qk, t + 1)
                    if t >= 2:
                        dve.wait_ge(s_exp, t - 1)
                    for b in range(2):
                        ins = nc.vector.reduce_max(mx[:, i, 2 * b:2 * b + 2],
                                                   bank[(4, 0)[i] + b][:, :].rearrange("p (c k) -> p c k", c=2),
                                                   axis=AX.X)
                    link(ins)
                    link(nc.vector.scalar_tensor_tensor(out=m_row[:, :], in0=mx[:, i, :], scalar=HD ** -0.5,
                                                        in1=sinks, op0=ALU.mult, op1=ALU.max))
                    nc.vector.tensor_scalar(neg_m[:, i, :], m_row[:, :], -1.0, None, ALU.mult)
                    nc.vector.tensor_tensor(sink_in[:, i, :], sinks, m_row[:, :], ALU.subtract).then_inc(s_m, 1)

                def normalise(t):
                    i = t % 2
                    dve.wait_ge(s_exp, t + 1)
                    link(nc.vector.tensor_tensor(den[:, :], row_sum[:, i, :], sink_e[:, i, :], ALU.add))
                    link(nc.vector.reciprocal(den[:, :], den[:, :]))
                    for j in range(4):
                        ins = nc.vector.tensor_scalar(prob[i][:, j, :], prob[i][:, j, :], den[:, j:j + 1], None,
                                                      ALU.mult)
                    ins.then_inc(s_p, 1)

                def copy_own(t):
                    dve.wait_ge(s_t, t + 1)
                    if t >= 2:
                        dve.wait_ge(s_pv, t - 1)
                    nc.vector.tensor_copy(probT[t % 2][:, 1, :], bank[7][:, :]).then_inc(s_tb, 1)

                def out_lo(t):
                    n, cp = divmod(t, 4)
                    at = slice(2 * cp, 2 * cp + 2), slice(n * P, (n + 1) * P)
                    dve.wait_ge(s_ohi, t + 1)
                    nc.vector.tensor_tensor(a_lo[:, at[0], at[1]],
                                            bank[2 + t % 2][:, 0:2 * P].rearrange("p (c q) -> p c q", c=2),
                                            a_hi[:, at[0], at[1]].bitcast(F32), ALU.subtract).then_inc(s_o, 1)

                steps = 4 * NB
                maxima(0)
                normalise(0)
                for t in range(steps):
                    if t + 1 < steps:
                        maxima(t + 1)
                    copy_own(t)
                    if t + 1 < steps:
                        normalise(t + 1)
                    if t:
                        out_lo(t - 1)
                out_lo(steps - 1)

            def conv(n0):
                def finish(j):
                    dve.wait_ge(s_cv, j + 1)
                    link(nc.vector.tensor_tensor(y[:, j, :], bank[6 + j % 2][:, :], y[:, j, :], ALU.add))
                    link(nc.vector.tensor_tensor(y[:, j, :], y[:, j, :], sq[:, j % 2, :], ALU.add))
                    if j == 0:
                        ins = nc.vector.tensor_copy(ss[:, :], y[:, 0, :])
                    else:
                        dve.wait_ge(s_y, j)
                        ins = nc.vector.tensor_tensor(ss[:, :], ss[:, :], y[:, j, :], ALU.add)
                    ins.then_inc(s_y, 1)

                for j in range(KD):
                    p = j % 2
                    for e in range(2):
                        n = n0 + 2 * j + e
                        next_slot(n, n % RING)
                        scale_to((U, G)[e][:, p, :], n % RING, n, 5)
                    if j == 0:
                        dve.wait_ge(s_memset, 5)
                    else:
                        dve.wait_ge(s_uhi, j - 1) if j > 1 else None
                    dve.wait_ge(s_sig, j + 1)
                    nc.vector.scalar_tensor_tensor(out=u[p][:, CW - 1:], in0=U[:, p, :], scalar=col("b_pw1", j),
                                                   in1=G[:, p, :], op0=ALU.add, op1=ALU.mult).then_inc(s_u, 1)
                    dve.wait_ge(s_u, j + 1)
                    sums = y[:, j, :], sq[:, p, :]
                    for i, w in enumerate(range(PE_TAPS, CW)):
                        out, src = sums[i % 2], u[p][:, w:w + T]
                        if i >= 2:
                            dve.wait_ge(s_dve, chain[0] - 1)
                        if i == 0:
                            ins = nc.vector.tensor_scalar(out, src, col("w_dw", j * CW + w), col("b_dw", j),
                                                          ALU.mult, ALU.add)
                        elif i == 1:
                            ins = nc.vector.tensor_scalar(out, src, col("w_dw", j * CW + w), None, ALU.mult)
                        else:
                            ins = nc.vector.scalar_tensor_tensor(out=out, in0=src, scalar=col("w_dw", j * CW + w),
                                                                 in1=out, op0=ALU.mult, op1=ALU.add)
                        ins.then_inc(s_dve, 1)
                        chain[0] += 1
                        if i == 2 * (CW - PE_TAPS) // 3:
                            dve.wait_ge(s_uhi, j + 1)
                            nc.vector.tensor_tensor(u_lo, u[p], u_hi.bitcast(F32), ALU.subtract).then_inc(s_ulo, 1)
                    dve.wait_ge(s_dve, chain[0])
                    if j:
                        finish(j - 1)
                finish(KD - 1)
                dve.wait_ge(s_mu, 1)
                for m in range(KD):
                    nc.vector.tensor_tensor(y[:, m, :], y[:, m, :], mean[:, :], ALU.subtract).then_inc(s_xc, 1)
                dve.wait_ge(s_lroot, 1)
                on_diagonals(s_ldiag)
                dve.wait_ge(s_lbc, 1)
                for m in range(KD):
                    nc.vector.tensor_tensor(y[:, m, :], y[:, m, :], BCAST[:, :], ALU.mult).then_inc(s_z, 1)
                    if m:
                        z_lo_of(m - 1)
                z_lo_of(KD - 1)

            def z_lo_of(m):
                dve.wait_ge(s_zhi, m + 1)
                nc.vector.tensor_tensor(a_lo[:, m, :], y[:, m, :], a_hi[:, m, :].bitcast(F32), ALU.subtract
                                        ).then_inc(s_zlo, 1)

            nc.vector.memset(ones[:, :], 1.0).then_inc(s_memset, 1)
            nc.vector.memset(eps[:, 0:1], EPS)
            link(nc.vector.memset(eps[:, 1:2], LN_EPS))
            dve.wait_ge(s_cols, 16)
            for sub in HALF_WEIGHT:
                at = cols[:, COLS["post"] + sub * KD:COLS["post"] + (sub + 1) * KD]
                ins = nc.vector.tensor_scalar(at, at, 0.5, None, ALU.mult)
            ins.then_inc(s_half, 1)
            dve.wait_ge(s_half, 1)
            for s in range(RING):
                w_lo_of(s, s)
            dve.wait_ge(s_dwhi, 1)
            nc.vector.tensor_tensor(dw_lo[:, :], cols[:, COLS["w_dw"]:COLS["w_dw"] + KD * CW],
                                    dw_hi[:, :].bitcast(F32), ALU.subtract).then_inc(s_dw, 1)
            for k in range(KD):
                x_lo_of(0, k)
                if 1 <= k <= KD - 2:
                    add_h_square(0, k)
            dve.wait_ge(s_const, CONSTS)
            invert(1)
            ffn(FFN0, 0, 0)
            qkv(QKV)
            attention()
            down(WO, "b_o", 1)
            boundary(1)
            ffn(FFN1, 1, 2)
            ffn(FFN2, 2, 3)
            conv(PW1)
            down(PW2, "b_pw2", 4)
            boundary(4)
            ffn(FFN3, 3, 5)


def up_slots(w):
    n = w.shape[1] // P
    return w.reshape(KD, P, n, P).transpose(2, 1, 0, 3).reshape(n, P, SLOT)


def down_slots(w):
    k = w.shape[0] // P
    out = np.zeros((KD, P, BLK, P), w.dtype)
    out[:, :, :k] = w.reshape(k, P, KD, P).transpose(2, 1, 0, 3)
    return out.reshape(KD, P, SLOT)


def ffn_slots(w_in, w_out):
    pairs = np.stack([up_slots(w_in[:, :FF]), up_slots(w_in[:, FF:])], 1)
    parts, c = [], 0
    for chunks in FFN_GROUPS:
        parts.append(pairs[c:c + chunks].reshape(2 * chunks, P, SLOT))
        parts.append(down_slots(w_out[c * P:(c + chunks) * P]))
        c += chunks
    return parts


def tables():
    pos = np.arange(T, dtype=np.float32)
    inv = np.float32(THETA) ** (-np.arange(0, ROT, 2, dtype=np.float32) / np.float32(ROT))
    ang = pos[None, :] * inv.astype(np.float32)[:, None]
    rc, rs = np.ones((P, T), np.float32), np.zeros((P, T), np.float32)
    perm = np.zeros((P, P), np.float32)
    r = ROT // 2
    for o in range(0, P, HD):
        rc[o:o + r] = rc[o + r:o + ROT] = np.cos(ang)
        rs[o:o + r], rs[o + r:o + ROT] = -np.sin(ang), np.sin(ang)
        for i in range(r):
            perm[o + i, o + r + i] = perm[o + r + i, o + i] = 1.0
    q, k = np.arange(P)[:, None], np.arange(2 * P)[None, :]
    diff = q + P - k
    band = (diff >= 0) & (diff < P)
    mask = np.zeros((P, 2, 2, 2 * P), np.float32)
    mask[:, 0] = np.where(band & (k >= P), 0.0, -1e30)[:, None]
    mask[:, 1] = np.where(band, 0.0, -1e30)[:, None]
    return rc, rs, perm, np.eye(P, dtype=np.float32), mask.reshape(P, 2, 4 * P)


def kernel(x, norm_pre, norm_post, w_ffn_in, w_ffn_out, attn_w_qkv, attn_b_qkv, attn_w_o, attn_b_o, attn_sinks,
           conv_w_pw1, conv_b_pw1, conv_w_dw, conv_b_dw, conv_ln_g, conv_ln_b, conv_w_pw2, conv_b_pw2):
    import concourse.bacc as bacc
    import ml_dtypes
    from concourse.bass_utils import run_bass_kernel_spmd

    given = dict(locals())
    (x, norm_pre, norm_post, w_ffn_in, w_ffn_out, w_qkv, b_qkv, w_o, b_o, sinks, w_pw1, b_pw1, w_dw, b_dw, ln_g, ln_b,
     w_pw2, b_pw2) = (np.asarray(given[n]) for n in kernel.__code__.co_varnames[:kernel.__code__.co_argcount])

    heads = [head_of(c // 2, b, c % 2) for c in range(KD) for b in range(2)]
    q_cols = np.concatenate([np.arange(hd * HD, (hd + 1) * HD) for hd in heads])
    q_dim, kv_dim = HEADS * HD, KV * HD
    qk_cols = np.concatenate([q_dim + np.arange(kv_dim), q_cols])
    w_v = w_qkv[0][:, q_dim + kv_dim:].reshape(2, 4, P, kv_dim).transpose(0, 2, 1, 3).reshape(2, P, SLOT)
    pw1 = np.stack([up_slots(w_pw1[0][:, :D]), up_slots(w_pw1[0][:, D:])], 1).reshape(2 * KD, P, SLOT)
    stream = np.concatenate(
        ffn_slots(w_ffn_in[0, 0], w_ffn_out[0, 0])
        + [up_slots(w_qkv[0][:, qk_cols]), w_v, down_slots(w_o[0][q_cols])]
        + ffn_slots(w_ffn_in[0, 1], w_ffn_out[0, 1]) + ffn_slots(w_ffn_in[1, 0], w_ffn_out[1, 0])
        + [pw1, down_slots(w_pw2[0])] + ffn_slots(w_ffn_in[1, 1], w_ffn_out[1, 1]))

    def cols(v):
        return v.reshape(-1, P).T

    sink_order = [head_of(cp, b, cc) for cp in range(4) for b in range(2) for cc in range(2)]
    col_in = np.concatenate(
        [cols(norm_pre), cols(norm_post), cols(b_qkv[0][qk_cols]), cols(b_o), cols(b_pw1), cols(b_dw), cols(ln_g),
         cols(ln_b), cols(b_pw2), w_dw[0].reshape(CW, KD, P).transpose(2, 1, 0).reshape(P, KD * CW),
         np.broadcast_to(sinks[0][sink_order], (P, HEADS)), np.broadcast_to(b_qkv[0][q_dim + kv_dim:], (P, kv_dim))], 1)
    rc, rs, perm, ident, mask = tables()
    bf = ml_dtypes.bfloat16
    ins = {"stream": stream, "xT": np.ascontiguousarray(x[0].T), "cols_in": np.ascontiguousarray(col_in),
           "rope_c": rc, "rope_s": rs, "perm_in": perm, "ident_in": ident, "ident_b_in": ident.astype(bf),
           "mask_in": mask.astype(bf)}

    nc = bacc.Bacc("TRN2", target_bir_lowering=False, num_devices=1)
    args = [nc.dram_tensor(n, a.shape, mybir.dt.from_np(a.dtype), kind="ExternalInput").ap() for n, a in ins.items()]
    out = nc.dram_tensor("outT", (D, T), F32, kind="ExternalOutput").ap()
    build_program(nc, *args, out)
    r = run_bass_kernel_spmd(nc, [ins], core_ids=[0])
    return np.ascontiguousarray(r.results[0]["outT"].T)[None]
```

```python
from contextlib import ExitStack

import numpy as np

import concourse.bass as bass
from concourse import mybir

F32 = mybir.dt.float32
F32R = mybir.dt.float32r
BF16 = mybir.dt.bfloat16
ALU = mybir.AluOpType
ACT = mybir.ActivationFunctionType
AX = mybir.AxisListType

P = 128
D = 1024
T = 512
KD = D // P
FF = 2816
KF = FF // P
FFN_GROUPS = (8, 8, 6)
HEADS, KV, HD = 16, 4, 64
GROUP = HEADS // KV
ROT, THETA = HD // 4, 500000.0
NB = T // P
CW = 31
RING = 4
BLK = 8
SLOT = BLK * P
EPS, LN_EPS = 1e-6, 1e-5
PH = 4
NT = T // PH
GC = P // PH
GROUPS = P // GC
SHIFTS = (CW - 2 + PH) // PH + 1
PAD = SHIFTS - 1
TAPS = SHIFTS * PH
EARLY = 4
SUBS = 6
HALF_WEIGHT = (0, 2, 3, 5)

FFN_SLOTS = 2 * KF + KD * len(FFN_GROUPS)
QKV_SLOTS, DOWN_SLOTS, PW1_SLOTS = 12, KD, 2 * KD
FFN0 = 0
QKV = FFN0 + FFN_SLOTS
WO = QKV + QKV_SLOTS
FFN1 = WO + DOWN_SLOTS
FFN2 = FFN1 + FFN_SLOTS
PW1 = FFN2 + FFN_SLOTS
PW2 = PW1 + PW1_SLOTS
FFN3 = PW2 + DOWN_SLOTS
SLOTS = FFN3 + FFN_SLOTS

COLS, _at = {}, 0
for _name, _n in (("pre", SUBS * KD), ("post", SUBS * KD), ("b_qk", 10), ("b_o", KD), ("b_pw1", 2 * KD),
                  ("ln_g", KD), ("ln_b", KD), ("b_pw2", KD),
                  ("sinks", HEADS), ("b_v", KV * HD)):
    COLS[_name] = _at
    _at += _n
N_COLS = _at


def head_of(cp, b, cc):
    c = 2 * cp + cc
    return (2 * (c // GROUP) + b) * GROUP + c % GROUP


def build_program(nc, stream, xT, cols_in, rope_c, rope_s, perm_in, ident_in, ident_b_in, mask_in, taps_in, conv_in,
                  u_dram, z_dram, outT):
    ctx = ExitStack()
    with ctx:
        def sb(name, shape, dt=F32):
            return ctx.enter_context(nc.sbuf_tensor(name, shape, dt))

        def sem(name):
            return ctx.enter_context(nc.semaphore(name))

        h = sb("h_resid", [P, KD, T])
        x_hi, x_lo = sb("x_hi", [P, KD, T], F32R), sb("x_lo", [P, KD, T], F32R)
        a_hi, a_lo = sb("a_hi", [P, BLK, T], F32R), sb("a_lo", [P, BLK, T], F32R)
        f = sb("f_out", [P, KD, T])
        raw = sb("w_raw", [P, RING, SLOT])
        w_hi, w_lo = sb("w_hi", [P, RING, SLOT], F32R), sb("w_lo", [P, RING, SLOT], F32R)
        G, U = sb("gate_tmp", [P, 2, T]), sb("up_tmp", [P, 2, T])
        ss = sb("sum_sq", [P, T])
        sq = sb("sq_tmp", [P, 2, T])
        r_pre = sb("r_pre", [P, T])
        cols = sb("cols", [P, N_COLS])
        rc, rs = sb("rope_cos", [P, T]), sb("rope_sin", [P, T])
        perm, ident = sb("rope_perm", [P, P]), sb("ident", [P, P])
        ident_b, mask = sb("ident_b", [P, P], BF16), sb("mask", [P, 2, 2 * P], BF16)
        ones = sb("ones", [P, P])
        eps, tiny = sb("eps", [P, 2]), sb("tiny", [P, 2])
        qT = sb("qT", [P, KD, T])
        kT = sb("kT", [P, 2, T])
        V = sb("V", [P, NB, KV * HD])
        r_col, root_col = sb("r_col", [P, NB]), sb("root_col", [P, NB])
        mx, m_row, neg_m = sb("mx", [P, 2, 4]), sb("m_row", [P, 4]), sb("neg_m", [P, 2, 4])
        sink_in, sink_e = sb("sink_in", [P, 2, 4]), sb("sink_e", [P, 2, 4])
        row_sum, den = sb("row_sum", [P, 2, 4]), sb("den", [P, 4])
        fv = f[:, :, :].rearrange("p a n -> p (a n)")
        prob = [fv[:, i * 1024:(i + 1) * 1024].rearrange("p (j k) -> p j k", j=4) for i in range(2)]
        probT = [fv[:, 2048 + i * 1024:2048 + (i + 1) * 1024].rearrange("p (kb c) -> p kb c", kb=2)
                 for i in range(2)]
        Vf = V[:, :, :].rearrange("p a n -> p (a n)")
        u = [Vf[:, i * T:(i + 1) * T] for i in range(2)]
        ug = sb("u_groups", [P, 2, GROUPS, PAD + NT])
        taps = sb("taps", [P, 2, GROUPS, SHIFTS, PH])
        conv_c = sb("conv_consts", [P, GC + P + KD * GROUPS])
        same_c, same_q, b_dw = conv_c[:, 0:GC], conv_c[:, GC:GC + P], conv_c[:, GC + P:]
        extra = sb("tap_matrix", [P, SHIFTS * P])
        flat = (fv[:, i * SHIFTS * P:(i + 1) * SHIFTS * P] for i in range(KD * T // (SHIFTS * P)))
        mats = [m.rearrange("p (m c q) -> p m c q", m=SHIFTS, c=GC) for m in (*flat, extra[:, :])]
        kf = kT[:, :, :].rearrange("p a n -> p (a n)")
        zg = [z.rearrange("p (g n) -> p g n", g=GROUPS) for z in (kf[:, 0:T], kf[:, T:2 * T], rc[:, :], rs[:, :])]
        zsq = [z.rearrange("p (g n) -> p g n", g=GROUPS) for z in (G[:, 0, :], U[:, 0, :], ss[:, :])]
        m0, dl, var = sb("mean_early", [P, NT]), sb("mean_rest", [P, NT]), sb("var", [P, NT])
        dl_sq, std = m0, var
        early = sq[:, 0, :].rearrange("p (j n) -> p j n", j=EARLY)
        dl_diag, std_diag = G[:, 1, :], U[:, 1, :]
        y = qT
        diag = sq[:, 0, :].rearrange("p (t c) -> p t c", t=NB)

        bank = [ctx.enter_context(nc.psum_tensor(f"bank{i}", [P, T], F32)) for i in range(8)]
        STAT, BCAST = bank[4], bank[5]
        OUT_BANKS = 0, 1, 2, 3
        PE_OUT = len(OUT_BANKS)
        gains = [G[:, :, :].rearrange("p a n -> p (a n)")[:, k * P:(k + 1) * P] for k in range(PE_OUT)]

        def keys(n):
            return 2 * P if n else P

        def scored(out, n):
            return out[:, 0:2 * keys(n)].rearrange("p (c k) -> p c k", c=2)

        def v_out(t):
            return bank[2 + t // 2][:, t % 2 * 2 * P:(t % 2 + 1) * 2 * P]

        s_raw = [sem(f"raw_loaded{i}") for i in range(RING)]
        s_h0 = [sem(f"x_loaded{k}") for k in range(KD)]
        s_const, s_cols = sem("consts_loaded"), sem("cols_loaded")
        s_ones, s_zeros = sem("ones_written"), sem("zeros_written")
        s_hi, s_lo = sem("weight_hi"), sem("weight_lo")
        s_raw0 = [sem(f"first_raw_loaded{i}") for i in range(RING)]
        s_hi0, s_lo0 = sem("first_weight_hi"), sem("first_weight_lo")
        s_mm = sem("slot_multiplied")
        s_mm0, s_evac0 = sem("first_half_multiplied"), sem("first_half_evacuated")
        s_evac = sem("slot_evacuated")
        s_half = sem("post_gain_halved")
        s_xhi, s_x = sem("x_hi_ready"), sem("x_ready")
        s_hsq, s_hacc = sem("h_squared"), sem("h_sq_added")
        s_fsq, s_facc = sem("f_squared"), sem("f_sq_added")
        s_h = sem("h_updated")
        s_stat, s_root, s_diag = sem("sum_sq_done"), sem("root_done"), sem("rms_inverted")
        s_bc, s_rpre = sem("rms_broadcast"), sem("r_pre_ready")
        s_act, s_prod, s_ahi, s_a = sem("gate_activated"), sem("gate_times_up"), sem("a_hi_ready"), sem("a_ready")
        s_dve = sem("vector_chain")
        s_qb, s_perm, s_rope = sem("qk_biased"), sem("qk_permuted"), sem("qk_rotated")
        s_v = sem("v_ready")
        s_qk, s_m, s_exp, s_p = sem("scores_ready"), sem("max_ready"), sem("exp_done"), sem("probs_ready")
        s_t, s_ta, s_tb = sem("probs_transposed"), sem("probT_prev"), sem("probT_own")
        s_pv, s_ohi, s_o = sem("pv_done"), sem("o_hi_ready"), sem("o_ready")
        s_sig, s_u = sem("gate_sigmoid"), sem("u_ready")
        s_taps = [sem(f"taps_loaded{i}") for i in range(2)]
        s_ud = [sem(f"u_in_dram{i}") for i in range(2)]
        s_ug = [sem(f"u_groups_loaded{i}") for i in range(2)]
        s_zd = [sem(f"z_in_dram{i}") for i in range(4)]
        s_y = [sem(f"y_loaded{j}") for j in range(KD)]
        s_mat, s_cv, s_zg = sem("tap_matrix_ready"), sem("group_convolved"), sem("z_groups_ready")
        s_early = sem("early_groups_added")
        s_m0mm, s_m0, s_zc = sem("early_mean_summed"), sem("early_mean_ready"), sem("z_centred")
        s_zsq, s_sqmm, s_dlmm = sem("z_squared"), sem("z_sq_summed"), sem("rest_summed")
        s_dl, s_dldiag, s_var = sem("rest_mean_ready"), sem("rest_mean_spread"), sem("var_ready")
        s_lroot, s_ldiag, s_lbc = sem("std_ready"), sem("std_inverted"), sem("mean_and_std_broadcast")
        s_z, s_zact, s_zhi, s_zlo = sem("z_normalised"), sem("z_activated"), sem("z_hi_ready"), sem("z_lo_ready")
        s_out = sem("out_stored")
        s_fsq0 = sem("first_half_squared")
        s_gain, s_fn = sem("gains_ready"), sem("f_normalised")
        s_sum, s_final = sem("residual_summed"), sem("output_ready")

        HALVES = slice(0, T // 2), slice(T // 2, T)

        def col(name, i):
            return cols[:, COLS[name] + i:COLS[name] + i + 1]

        def blk(ring, s, k, width=P):
            return ring[:, s, k * width:(k + 1) * width]

        block = ctx.enter_context(nc.Block())

        @block.sync
        def _(sp):
            def first_slots(half, done):
                at = slice(half * SLOT // 2, (half + 1) * SLOT // 2)
                for s in range(RING):
                    sp.dma_start(raw[:, s, at], stream[s, :, at]).then_inc(done[s], 16)

            def x_chunks(k0, k1):
                for k in range(k0, k1):
                    sp.dma_start(h[:, k, :], xT[k * P:(k + 1) * P, :]).then_inc(s_h0[k], 16)

            sp.dma_start(cols[:, :], cols_in[:, :]).then_inc(s_cols, 16)
            x_chunks(0, 1)
            first_slots(0, s_raw0)
            x_chunks(1, KD // 2)
            first_slots(1, s_raw)
            x_chunks(KD // 2, KD)

            def load(n, s):
                sp.wait_ge(s_lo, n + (1 - RING))
                sp.dma_start(raw[:, s, :], stream[bass.ds(n, 1), :, :].rearrange("a p n -> p (a n)")
                             ).then_inc(s_raw[s], 16)

            def loads(turn0, turn1):
                with sp.Fori(turn0, turn1) as i:
                    for s in range(RING):
                        load(RING * i + s, s)

            def by_groups(dram, j):
                return dram[j, :, :].rearrange("(g c) (q n) -> (c q) g n", g=GROUPS, q=PH)

            def load_taps(j):
                if j >= 2:
                    sp.wait_ge(s_mat, GROUPS * (j - 1))
                sp.dma_start(taps[:, j % 2, :, :, :].rearrange("p g m q -> p (g m q)"), taps_in[j, :, :]
                             ).then_inc(s_taps[j % 2], 16)

            def store_u(j):
                sp.wait_ge(s_u, j + 1)
                sp.dma_start(u_dram[j, :, :], u[j % 2]).then_inc(s_ud[j % 2], 16)

            def load_groups(j):
                sp.wait_ge(s_ud[j % 2], 16 * (j // 2 + 1))
                if j >= 2:
                    sp.wait_ge(s_cv, GROUPS * (j - 1))
                sp.dma_start(ug[:, j % 2, :, PAD:], by_groups(u_dram, j)).then_inc(s_ug[j % 2], 16)

            def store_z(j):
                sp.wait_ge(s_zc, j + 1)
                sp.dma_start(by_groups(z_dram, j), zg[j % 4]).then_inc(s_zd[j % 4], 16)

            def load_y(j):
                sp.wait_ge(s_zd[j % 4], 16 * (j // 4 + 1))
                sp.dma_start(y[:, j, :], z_dram[j, :, :]).then_inc(s_y[j], 16)

            conv_turn = (PW1 + 2 * RING) // RING
            loads(1, conv_turn)
            load_taps(0)
            load_taps(1)
            for j in range(KD):
                n = PW1 + 2 * RING + 2 * j
                load(n, n % RING)
                if j == KD - 1:
                    load_y(4)
                    store_z(5)
                load(n + 1, (n + 1) % RING)
                if 2 <= j < KD - 1:
                    load_taps(j)
                store_u(j)
                if j == KD - 2:
                    for i in range(4):
                        store_z(i)
                if j == KD - 1:
                    load_y(5)
                load_groups(j)
                if j == KD - 2:
                    for i in range(4):
                        load_y(i)
                    load_taps(KD - 1)
                    store_z(4)
            store_z(6)
            load_y(6)
            store_z(7)
            load_y(7)
            loads(conv_turn + PW1_SLOTS // RING, SLOTS // RING)
            for m in range(KD):
                if m < PE_OUT:
                    sp.wait_ge(s_final, m + 1)
                else:
                    sp.wait_ge(s_h, (SUBS - 1) * KD + m - PE_OUT + 1)
                sp.dma_start(outT[m * P:(m + 1) * P, :], h[:, m, :]).then_inc(s_out, 16)
            sp.wait_ge(s_out, 16 * KD)

        @block.gpsimd
        def _(pool):
            pool.wait_ge(s_h0[KD - 1], 16)
            for dst, src in ((ident_b, ident_b_in), (ident, ident_in), (rc, rope_c), (rs, rope_s), (perm, perm_in)):
                pool.dma_start(dst[:, :], src[:, :]).then_inc(s_const, 16)
            pool.dma_start(mask[:, :, :], mask_in[:, :, :]).then_inc(s_const, 16)
            pool.dma_start(conv_c[:, :], conv_in[:, :]).then_inc(s_const, 16)
            for i in range(2):
                nc.gpsimd.memset(ug[:, i, :, 0:PAD], 0.0).then_inc(s_zeros, 1)

        CONSTS = 7 * 16

        @block.tensor
        def _(pe):
            def mm3(out, lw, lx, first, last):
                nc.tensor.matmul(out, lw[0], lx[0], start=first, stop=False)
                nc.tensor.matmul(out, lw[0], lx[1], start=False, stop=False)
                return nc.tensor.matmul(out, lw[1], lx[0], start=False, stop=last)

            def x_block(s, k, last=KD - 1):
                return mm3(bank[s][:, :], (blk(w_hi, s, k), blk(w_lo, s, k)), (x_hi[:, k, :], x_lo[:, k, :]),
                           k == 0, k == last)

            def keep_warm(count, out=7):
                for _ in range(count):
                    nc.tensor.matmul(bank[out][:, :], ident_b[:, :], mask[:, :, :], start=True, stop=True)

            def add_columns(src, first, last, blocks=range(NB)):
                for t in blocks:
                    ins = nc.tensor.matmul(STAT[:, t:t + 1], src[:, t * P:(t + 1) * P], ones[:, 0:1],
                                           start=(first and t == 0), stop=last, skip_group_check=True)
                return ins

            def broadcast():
                return nc.tensor.matmul(BCAST[:, :], ones[:, :], sq[:, 0, :],
                                        start=True, stop=True)

            def four_slots(n0, blocks, hi_ready, lo_ready, before_last, among_last):
                x = {KD: (x_hi, x_lo), -KD: (a_hi, a_lo)}[blocks]
                for k in range(KD - 1):
                    pe.wait_ge(*hi_ready(k))
                    for s in range(RING):
                        if n0 == 0 and k == 0:
                            pe.wait_ge(s_lo0, s + 1)
                        elif n0 == 0 and k == KD // 2:
                            pe.wait_ge(s_lo, s + 1)
                        elif k == 0:
                            pe.wait_ge(s_lo, n0 + s + 1)
                            pe.wait_ge(s_evac, n0 + s - RING + 1)
                        nc.tensor.matmul(bank[s][:, :], blk(w_hi, s, k), x[0][:, k, :], start=(k == 0), stop=False)
                        nc.tensor.matmul(bank[s][:, :], blk(w_lo, s, k), x[0][:, k, :], start=False, stop=False)
                    pe.wait_ge(*lo_ready(k))
                    for s in range(RING):
                        nc.tensor.matmul(bank[s][:, :], blk(w_hi, s, k), x[1][:, k, :], start=False, stop=False)
                before_last()
                pe.wait_ge(*lo_ready(KD - 1))
                for s in range(RING):
                    if s == 2:
                        among_last()
                    mm3(bank[s][:, :], (blk(w_hi, s, KD - 1), blk(w_lo, s, KD - 1)),
                        (x[0][:, KD - 1, :], x[1][:, KD - 1, :]), False, True).then_inc(s_mm, 1)

            def first_body(n0, sub):
                def columns():
                    if sub:
                        pe.wait_ge(s_root, 2 * sub)
                    pe.wait_ge(s_hacc, (KD - 2) * sub + KD - 2)
                    add_columns(f[:, 0, :], True, False)
                    pe.wait_ge(s_hsq, KD * sub + KD)
                    add_columns(f[:, KD - 1, :], False, True).then_inc(s_stat, 1)

                def spread():
                    pe.wait_ge(s_diag, 2 * sub + 1)
                    if sub:
                        pe.wait_ge(s_h, KD * sub)
                    broadcast().then_inc(s_bc, 1)

                four_slots(n0, KD, lambda k: (s_xhi, KD * sub + k + 1), lambda k: (s_x, KD * sub + k + 1),
                           columns, spread)

            def body(n, s):
                pe.wait_ge(s_lo, n + 1)
                pe.wait_ge(s_evac, n + (1 - RING))
                for k in range(KD):
                    last = x_block(s, k)
                last.then_inc(s_mm, 1)

            def bodies(n0, count):
                with pe.Fori(0, count // RING) as i:
                    for s in range(RING):
                        body(RING * i + (n0 + s), s)

            def down_slot(n, s, blocks=KD, ready=None):
                pe.wait_ge(s_lo, n + 1)
                pe.wait_ge(s_evac, n + (1 - RING))
                for k in range(blocks):
                    if ready:
                        pe.wait_ge(*ready(k))
                    last = mm3(bank[s][:, :], (blk(w_hi, s, k), blk(w_lo, s, k)),
                               (a_hi[:, k, :], a_lo[:, k, :]), k == 0, k == blocks - 1)
                last.then_inc(s_mm, 1)

            def last_slot(n, s, blocks=KD):
                pe.wait_ge(s_lo, n + 1)
                pe.wait_ge(s_evac, n + (1 - RING))
                for half, tok in enumerate(HALVES):
                    for k in range(blocks):
                        last = mm3(bank[(6, s)[half]][:, tok], (blk(w_hi, s, k), blk(w_lo, s, k)),
                                   (a_hi[:, k, tok], a_lo[:, k, tok]), k == 0, k == blocks - 1)
                    last.then_inc((s_mm0, s_mm)[half], 1)

            def down(n0, blocks, ready, final):
                turns = KD // RING
                with pe.Fori(0, turns - 1 if final else turns) as i:
                    for s in range(RING):
                        down_slot(RING * i + (n0 + s), s, blocks, ready if s == 0 else None)
                if final:
                    for s in range(RING - 1):
                        down_slot(n0 + KD - RING + s, s, blocks)
                    last_slot(n0 + KD - 1, RING - 1, blocks)

            def post_stat(sub):
                if sub == 0:
                    pe.wait_ge(s_const, CONSTS)
                pe.wait_ge(s_root, 2 * sub + 1)
                pe.wait_ge(s_facc, (KD - 2) * (sub + 1))
                add_columns(ss, True, False)
                pe.wait_ge(s_fsq0, sub + 1)
                add_columns(sq[:, 1, :], False, False, range(NB // 2))
                pe.wait_ge(s_fsq, KD * (sub + 1))
                add_columns(sq[:, 1, :], False, True, range(NB // 2, NB)).then_inc(s_stat, 1)
                if sub == SUBS - 1:
                    pe.wait_ge(s_evac, SLOTS)
                    add_residual(0, 1)
                else:
                    keep_warm(6)
                pe.wait_ge(s_diag, 2 * sub + 2)
                pe.wait_ge(s_rpre, sub + 1)
                broadcast().then_inc(s_bc, 1)
                if sub < SUBS - 1:
                    keep_warm(10)

            def add_residual(k0, k1):
                for k in range(k0, k1):
                    nc.tensor.matmul(bank[OUT_BANKS[k]][:, :], ident[:, :], h[:, k, :], start=True, stop=False)

            def output():
                add_residual(1, PE_OUT)
                pe.wait_ge(s_gain, 1)
                for k in range(PE_OUT):
                    pe.wait_ge(s_fn, k + 1)
                    nc.tensor.matmul(bank[OUT_BANKS[k]][:, :], gains[k], f[:, k, :], start=False, stop=True
                                     ).then_inc(s_sum, 1)

            def ffn(n0, index, sub):
                n, q = n0, KF * index
                for g, chunks in enumerate(FFN_GROUPS):
                    if g == 0:
                        first_body(n, sub)
                        bodies(n + RING, 2 * chunks - RING)
                    else:
                        bodies(n, 2 * chunks)
                    n += 2 * chunks
                    down(n, chunks, lambda k, q=q: (s_a, q + k + 1), g == len(FFN_GROUPS) - 1)
                    n += KD
                    q += chunks
                post_stat(sub)

            def qkv(n0, sub):
                first_body(n0, sub)
                pe.wait_ge(s_const, CONSTS)

                def permute(c):
                    pe.wait_ge(s_qb, c + 1)
                    if c >= 2:
                        pe.wait_ge(s_rope, c - 1)
                    src = kT[:, c, :] if c < 2 else qT[:, c - 2, :]
                    nc.tensor.matmul(bank[6 + c % 2][:, :], perm[:, :], src, start=True, stop=True
                                     ).then_inc(s_perm, 1)

                after = {4: (0, 1), 5: (2, 3), 6: (4, 5), 7: (6,), 8: (7,), 9: (8,)}
                for c in range(RING, 10):
                    body(n0 + c, c % RING)
                    for j in after[c]:
                        permute(j)
                for half in range(2):
                    n, s = n0 + 10 + half, 2 + half
                    pe.wait_ge(s_lo, n + 1)
                    for t in range(NB):
                        if half == 0 and t % 2 == 0:
                            pe.wait_ge(s_evac, n0 + 7 + t // 2)
                        for kk in range(4):
                            k = 4 * half + kk
                            tok = slice(t * P, (t + 1) * P)
                            w, w_rest = blk(w_hi, s, kk, 2 * P), blk(w_lo, s, kk, 2 * P)
                            passes = (x_hi[:, k, tok], w), (x_hi[:, k, tok], w_rest), (x_lo[:, k, tok], w)
                            for i, (left, right) in enumerate(passes):
                                last = nc.tensor.matmul(v_out(t), left, right, start=(t % 2 == 0 and k == 0 and i == 0),
                                                        stop=(k == KD - 1 and i == 2), skip_group_check=True)
                    last.then_inc(s_mm, 1)
                    if half == 0:
                        permute(9)
                        scores(0)
                        scores(1)

            def scores(t):
                n, cp = divmod(t, 4)
                if t < 4:
                    pe.wait_ge(s_rope, 2 + 2 * (cp + 1))
                if t == 0:
                    pe.wait_ge(s_rpre, 2)
                if t == 1:
                    pe.wait_ge(s_evac, QKV + 10)
                if t >= 2:
                    pe.wait_ge(s_exp, t - 1)
                for b in range(2):
                    out = bank[(4, 0)[t % 2] + b]
                    nc.tensor.matmul(scored(out, n), ident_b[:, :], mask[:, :, 2 * P - keys(n):],
                                     start=True, stop=False)
                    for cc in range(2):
                        c, half = 2 * cp + cc, slice(b * HD, (b + 1) * HD)
                        last = nc.tensor.matmul(scored(out, n)[:, cc, :],
                                                qT[half, c, n * P:(n + 1) * P],
                                                kT[half, c // GROUP, (n + 1) * P - keys(n):(n + 1) * P],
                                                start=False, stop=(cc == 1))
                last.then_inc(s_qk, 1)

            def attention():
                def transposes(t):
                    if t > NB:
                        pe.wait_ge(s_ta, t - NB)
                    if t:
                        pe.wait_ge(s_tb, t)
                    if t == steps - 2:
                        keep_warm(4)
                    if 0 < t < NB:
                        keep_warm(2)
                    if t == 0:
                        pe.wait_ge(s_rope, 10)
                    pe.wait_ge(s_p, t + 1)
                    for kb in range(0 if t >= NB else 1, 2):
                        for j in range(4):
                            last = nc.tensor.transpose(bank[6 + kb][:, j * P:(j + 1) * P],
                                                       prob[t % 2][:, j, kb * P:(kb + 1) * P], ident[:, :])
                    last.then_inc(s_t, 1)

                def values(t):
                    n, cp = divmod(t, 4)
                    kc = cp // 2
                    if n:
                        pe.wait_ge(s_ta, t + 1 - NB)
                    pe.wait_ge(s_tb, t + 1)
                    if t == 0:
                        pe.wait_ge(s_v, 2)
                        pe.wait_ge(s_evac, QKV + QKV_SLOTS)
                    if t >= 2:
                        pe.wait_ge(s_o, t - 1)
                    for b in range(2):
                        for kb in range(0 if n else 1, 2):
                            kv = 2 * kc + b
                            last = nc.tensor.matmul(bank[2 + t % 2][b * HD:(b + 1) * HD, 0:2 * P],
                                                    V[:, n - 1 + kb, kv * HD:(kv + 1) * HD],
                                                    probT[t % 2][:, kb, b * 2 * P:(b + 1) * 2 * P],
                                                    start=(kb == (0 if n else 1)), stop=(kb == 1))
                    last.then_inc(s_pv, 1)

                def out_product(k0, k1):
                    for k in range(k0, k1):
                        if k == 0:
                            pe.wait_ge(s_exp, steps)
                        if k % 2 == 0:
                            pe.wait_ge(s_o, steps - 4 + k // 2 + 1)
                        for s in range(2):
                            if k == 0:
                                pe.wait_ge(s_lo, WO + s + 1)
                            last = mm3(bank[s][:, :], (blk(w_hi, s, k), blk(w_lo, s, k)),
                                       (a_hi[:, k, :], a_lo[:, k, :]), k == 0, k == KD - 1)
                            if k == KD - 1:
                                last.then_inc(s_mm, 1)

                steps = 4 * NB
                for t in range(steps):
                    if t + 2 < steps:
                        scores(t + 2)
                    if t:
                        values(t - 1)
                    transposes(t)
                    if t == steps - 2:
                        out_product(0, 2)
                    if t == steps - 1:
                        out_product(2, 4)
                values(steps - 1)
                out_product(4, KD)
                for m in range(2, KD - 1):
                    down_slot(WO + m, m % RING)
                last_slot(WO + KD - 1, RING - 1)

            def convolution(n0, sub):
                def convolve(j):
                    pe.wait_ge(s_ug[j % 2], 16 * (j // 2 + 1))
                    if j == 0:
                        pe.wait_ge(s_zeros, 2)
                    if j >= 2:
                        pe.wait_ge(s_zg, j - 1)
                    for g in range(GROUPS):
                        pe.wait_ge(s_mat, GROUPS * j + g + 1)
                        for m in range(SHIFTS):
                            last = nc.tensor.matmul(bank[6 + j % 2][:, g * NT:(g + 1) * NT],
                                                    mats[g][:, m, :, :].rearrange("p c q -> p (c q)"),
                                                    ug[:, j % 2, g, m:m + NT], start=(m == 0), stop=(m == PAD))
                        last.then_inc(s_cv, 1)

                def sum_groups(out, src, first, last):
                    for g in range(GROUPS):
                        ins = nc.tensor.matmul(out[:, 0:NT], same_q, src[:, g, :], start=(first and g == 0),
                                               stop=(last and g == GROUPS - 1))
                    return ins

                def sum_early():
                    pe.wait_ge(s_rpre, sub + 1)
                    for j in range(EARLY):
                        pe.wait_ge(s_early, j + 1)
                        last = nc.tensor.matmul(BCAST[:, 0:NT], same_q, early[:, j, :], start=(j == 0),
                                                stop=(j == EARLY - 1))
                    last.then_inc(s_m0mm, 1)

                def sum_rest(j):
                    pe.wait_ge(s_zc, j + 1)
                    sum_groups(BCAST, zg[j % 4], j == EARLY, j == KD - 1).then_inc(s_dlmm, 1)

                def sum_squares(j):
                    if j == 0:
                        pe.wait_ge(s_root, 2 * sub + 1)
                    pe.wait_ge(s_zsq, j + 1)
                    sum_groups(STAT, zsq[j % 3], j == 0, j == KD - 1).then_inc(s_sqmm, 1)

                first_body(n0, sub)
                for j in range(2, KD - 2):
                    body(n0 + 2 * j, 2 * j % RING)
                    body(n0 + 2 * j + 1, (2 * j + 1) % RING)
                    convolve(j - 2)
                body(n0 + 12, 0)
                sum_early()
                body(n0 + 13, 1)
                convolve(4)
                body(n0 + 14, 2)
                convolve(5)
                for j in range(3):
                    sum_squares(j)
                body(n0 + 15, 3)
                convolve(6)
                for j in range(4, 6):
                    sum_rest(j)
                for j in range(3, 6):
                    sum_squares(j)
                convolve(7)
                for j in range(6, 8):
                    sum_rest(j)
                for j in range(6, 8):
                    sum_squares(j)

            def layer_norm():
                pe.wait_ge(s_dldiag, 1)
                nc.tensor.matmul(bank[6][:, :], ones[:, :], dl_diag, start=True, stop=True).then_inc(s_lbc, 1)
                keep_warm(8, out=5)
                pe.wait_ge(s_ldiag, 1)
                nc.tensor.matmul(bank[7][:, :], ones[:, :], std_diag, start=True, stop=True).then_inc(s_lbc, 1)
                keep_warm(11, out=5)
                four_slots(PW2, -KD, lambda k: (s_zhi, k + 1), lambda k: (s_zlo, k + 1),
                           lambda: None, lambda: None)
                for s in range(RING - 1):
                    down_slot(PW2 + RING + s, s)
                last_slot(PW2 + KD - 1, RING - 1)

            pe.wait_ge(s_ones, 1)
            ffn(FFN0, 0, 0)
            qkv(QKV, 1)
            attention()
            post_stat(1)
            ffn(FFN1, 1, 2)
            ffn(FFN2, 2, 3)
            convolution(PW1, 4)
            layer_norm()
            post_stat(4)
            ffn(FFN3, 3, 5)
            output()

        @block.scalar
        def _(act):
            def next_slot(n, s, turn):
                act.wait_ge(s_raw[s], 16 * turn + 32)
                act.wait_ge(s_mm, n + 1)
                nc.scalar.activation(w_hi[:, s, :], raw[:, s, :], ACT.Copy).then_inc(s_hi, 1)

            def x_chunk(sub, k):
                nc.scalar.activation(x_hi[:, k, :], h[:, k, :], ACT.Copy, scale=col("pre", sub * KD + k)
                                     ).then_inc(s_xhi, 1)
                nc.scalar.activation(f[:, k, :], h[:, k, :], ACT.Square).then_inc(s_hsq, 1)

            def root_of(stat_count):
                act.wait_ge(s_stat, stat_count)
                if stat_count > 1:
                    act.wait_ge(s_diag, stat_count - 1)
                nc.scalar.activation(root_col[:, :], STAT[:, 0:NB], ACT.Sqrt, bias=eps[:, 0:1], scale=1.0 / D
                                     ).then_inc(s_root, 1)

            def keep_r_pre(sub):
                act.wait_ge(s_bc, 2 * sub + 1)
                nc.scalar.activation(r_pre[:, :], BCAST[:, :], ACT.Copy).then_inc(s_rpre, 1)

            def sqrt_table():
                nc.scalar.activation(tiny[:, 0:1], eps[:, 0:1], ACT.Sqrt)

            def pair_steps(n, s, turn, q, chunk, first=False):
                if not first:
                    next_slot(n, s, turn)
                act.wait_ge(s_evac, n + 1)
                g = G[:, (s // 2) % 2, :]
                nc.scalar.activation(g, g, ACT.Silu).then_inc(s_act, 1)
                act.wait_ge(s_prod, q + 1)
                nc.scalar.activation(a_hi[:, chunk, :], U[:, (s // 2) % 2, :], ACT.Copy).then_inc(s_ahi, 1)
                next_slot(n + 1, s + 1, turn)

            def down(n0, last_of=None):
                if last_of is None:
                    with act.Fori(0, KD // RING) as i:
                        for s in range(RING):
                            next_slot(RING * i + (n0 + s), s, i + n0 // RING)
                    return
                sqrt_table()
                for m in range(KD):
                    n, s = n0 + m, m % RING
                    if n + RING < SLOTS and m < KD - 2:
                        next_slot(n, s, n // RING)
                    if m >= 3:
                        act.wait_ge(s_facc, (KD - 2) * last_of + m - 2)
                    if m == KD - 1:
                        act.wait_ge(s_evac0, last_of + 1)
                        nc.scalar.activation(sq[:, m % 2, HALVES[0]], f[:, m, HALVES[0]], ACT.Square
                                             ).then_inc(s_fsq0, 1)
                        act.wait_ge(s_evac, n + 1)
                        nc.scalar.activation(sq[:, m % 2, HALVES[1]], f[:, m, HALVES[1]], ACT.Square
                                             ).then_inc(s_fsq, 1)
                        continue
                    act.wait_ge(s_evac, n + 1)
                    nc.scalar.activation(ss[:, :] if m == 0 else sq[:, m % 2, :], f[:, m, :], ACT.Square
                                         ).then_inc(s_fsq, 1)
                    if n + RING < SLOTS and m == KD - 2:
                        next_slot(n, s, n // RING)

            def boundary(sub, n0):
                root_of(2 * sub + 2)
                if sub == SUBS - 1:
                    for k in range(PE_OUT):
                        ins = nc.scalar.activation(gains[k], ident[:, :], ACT.Copy, scale=col("post", sub * KD + k))
                    ins.then_inc(s_gain, 1)
                    for k in range(PE_OUT):
                        act.wait_ge(s_sum, k + 1)
                        nc.scalar.activation(h[:, k, :], bank[OUT_BANKS[k]][:, :], ACT.Copy).then_inc(s_final, 1)
                    return
                next_slot(n0 - 1, RING - 1, n0 // RING - 1)
                for k in range(KD):
                    act.wait_ge(s_h, KD * sub + k + 1)
                    x_chunk(sub + 1, k)
                root_of(2 * sub + 3)
                next_slot(n0, 0, n0 // RING)
                keep_r_pre(sub + 1)

            def ffn(n0, index, sub):
                n, q = n0, KF * index
                for g, chunks in enumerate(FFN_GROUPS):
                    if g == 0:
                        for p in range(2):
                            pair_steps(n + 2 * p, 2 * p, n // RING, q + p, p, first=(p == 0))
                    with act.Fori(1 if g == 0 else 0, 2 * chunks // RING) as i:
                        for p in range(2):
                            pair_steps(RING * i + (n + 2 * p), 2 * p, i + n // RING, 2 * i + (q + p),
                                       bass.ds(2 * i + p, 1))
                    n += 2 * chunks
                    down(n, sub if g == len(FFN_GROUPS) - 1 else None)
                    n += KD
                    q += chunks
                boundary(sub, n0 + FFN_SLOTS)

            def qkv(n0):
                for c in range(QKV_SLOTS):
                    n, s = n0 + c, c % RING
                    if 1 <= c < RING:
                        next_slot(n, s, n // RING)
                    if 1 <= c <= 10:
                        act.wait_ge(s_evac, n)
                        dst = kT[:, c - 1, :] if c <= 2 else qT[:, c - 3, :]
                        nc.scalar.activation(dst, G[:, (c - 1) % 2, :], ACT.Identity, bias=col("b_qk", c - 1)
                                             ).then_inc(s_qb, 1)
                    if c == QKV_SLOTS - 1:
                        exps(0)
                        exps(1)
                    if c >= RING:
                        next_slot(n, s, n // RING)

            def exps(t):
                act.wait_ge(s_m, t + 1)
                if t >= 2:
                    act.wait_ge(s_t, t - 1)
                for b in range(2):
                    for cc in range(2):
                        j = 2 * b + cc
                        nc.scalar.activation(prob[t % 2][:, j, 2 * P - keys(t // 4):],
                                             scored(bank[(4, 0)[t % 2] + b], t // 4)[:, cc, :], ACT.Exp,
                                             bias=neg_m[:, t % 2, j:j + 1], scale=HD ** -0.5,
                                             accum_out=row_sum[:, t % 2, j:j + 1])
                nc.scalar.activation(sink_e[:, t % 2, :], sink_in[:, t % 2, :], ACT.Exp).then_inc(s_exp, 1)

            def attention():
                def copy_prev(t):
                    act.wait_ge(s_t, t + 1)
                    if t >= 2:
                        act.wait_ge(s_pv, t - 1)
                    nc.scalar.activation(probT[t % 2][:, 0, :], bank[6][:, :], ACT.Copy).then_inc(s_ta, 1)

                def out_hi(t):
                    n, cp = divmod(t, 4)
                    act.wait_ge(s_pv, t + 1)
                    nc.scalar.activation(a_hi[:, 2 * cp:2 * cp + 2, n * P:(n + 1) * P],
                                         bank[2 + t % 2][:, 0:2 * P].rearrange("p (c q) -> p c q", c=2), ACT.Copy
                                         ).then_inc(s_ohi, 1)

                steps = 4 * NB
                for t in range(steps):
                    if 1 < t + 1 < steps:
                        exps(t + 1)
                    if t:
                        out_hi(t - 1)
                    if t >= NB:
                        copy_prev(t)
                out_hi(steps - 1)

            def conv(n0):
                def square(j):
                    act.wait_ge(s_zc, j + 1)
                    if j >= 3:
                        act.wait_ge(s_sqmm, j - 2)
                    nc.scalar.activation(zsq[j % 3], zg[j % 4], ACT.Square).then_inc(s_zsq, 1)

                for j in range(KD):
                    for e in range(2):
                        n = n0 + 2 * j + e
                        if n > n0:
                            next_slot(n, n % RING, n // RING)
                        if (j, e) == (KD - 1, 0):
                            act.wait_ge(s_u, KD - 1)
                            for i in range(3):
                                square(i)
                    act.wait_ge(s_evac, n + 1)
                    g = G[:, j % 2, :]
                    nc.scalar.activation(g, g, ACT.Sigmoid, bias=col("b_pw1", KD + j)).then_inc(s_sig, 1)
                sqrt_table()
                for j in range(3, KD):
                    square(j)
                act.wait_ge(s_var, 1)
                nc.scalar.activation(std[:, :], var[:, :], ACT.Sqrt, bias=eps[:, 1:2]).then_inc(s_lroot, 1)
                nc.scalar.activation(tiny[:, 1:2], eps[:, 0:1], ACT.Silu)
                for m in range(KD):
                    act.wait_ge(s_z, m + 1)
                    nc.scalar.activation(f[:, m, :].rearrange("p (n q) -> p q n", q=PH),
                                         y[:, m, :].rearrange("p (q n) -> p q n", q=PH), ACT.Silu,
                                         bias=col("ln_b", m), scale=col("ln_g", m)).then_inc(s_zact, 1)
                    act.wait_ge(s_zact, m + 1)
                    nc.scalar.activation(a_hi[:, m, :], f[:, m, :], ACT.Copy).then_inc(s_zhi, 1)

            act.wait_ge(s_ones, 1)
            sqrt_table()
            act.wait_ge(s_half, 1)
            for k in range(KD):
                act.wait_ge(s_h0[k], 16)
                x_chunk(0, k)
                if k in (0, 2):
                    at = slice(k // 2 * SLOT // 2, (k // 2 + 1) * SLOT // 2)
                    for s in range(RING):
                        act.wait_ge((s_raw0, s_raw)[k // 2][s], 16)
                        nc.scalar.activation(w_hi[:, s, at], raw[:, s, at], ACT.Copy
                                             ).then_inc((s_hi0, s_hi)[k // 2], 1)
            root_of(1)
            next_slot(0, 0, 0)
            keep_r_pre(0)
            ffn(FFN0, 0, 0)
            qkv(QKV)
            attention()
            down(WO, 1)
            boundary(1, FFN1)
            ffn(FFN1, 1, 2)
            ffn(FFN2, 2, 3)
            conv(PW1)
            down(PW2, 4)
            boundary(4, FFN3)
            ffn(FFN3, 3, 5)

        @block.vector
        def _(dve):
            chain = [0]

            def link(ins):
                chain[0] += 1
                ins.then_inc(s_dve, 1)
                dve.wait_ge(s_dve, chain[0])

            def next_slot(n, s):
                dve.wait_ge(s_hi, n + RING + 1)
                nc.vector.tensor_tensor(w_lo[:, s, :], raw[:, s, :], w_hi[:, s, :].bitcast(F32), ALU.subtract
                                        ).then_inc(s_lo, 1)

            def on_diagonals(done):
                link(nc.vector.reciprocal(r_col[:, :], root_col[:, :]))
                nc.vector.tensor_tensor(diag, ident[:, None, :].broadcast_to([P, NB, P]),
                                        r_col[:, :, None].broadcast_to([P, NB, P]), ALU.mult).then_inc(done, 1)

            def invert(count):
                dve.wait_ge(s_root, count)
                if count > 1:
                    dve.wait_ge(s_bc, count - 1)
                on_diagonals(s_diag)

            def x_lo_of(sub, k):
                dve.wait_ge(s_xhi, KD * sub + k + 1)
                nc.vector.scalar_tensor_tensor(out=x_lo[:, k, :], in0=h[:, k, :], scalar=col("pre", sub * KD + k),
                                               in1=x_hi[:, k, :].bitcast(F32), op0=ALU.mult, op1=ALU.subtract
                                               ).then_inc(s_x, 1)

            def add_h_square(sub, k):
                dve.wait_ge(s_hsq, KD * sub + k + 1)
                if k > 1:
                    dve.wait_ge(s_hacc, (KD - 2) * sub + k - 1)
                nc.vector.tensor_tensor(f[:, 0, :], f[:, 0, :], f[:, k, :], ALU.add).then_inc(s_hacc, 1)

            def scale_to(dst, s, n, rpre=None):
                dve.wait_ge(s_mm, n + 1)
                if rpre:
                    dve.wait_ge(s_rpre, rpre)
                nc.vector.tensor_tensor(dst, bank[s][:, :], r_pre[:, :], ALU.mult).then_inc(s_evac, 1)

            def pair_steps(n, s, q, chunk, rpre, first=False):
                p = (s // 2) % 2
                if not first:
                    next_slot(n, s)
                scale_to(G[:, p, :], s, n, rpre)
                scale_to(U[:, p, :], s + 1, n + 1)
                dve.wait_ge(s_evac, n + 2)
                dve.wait_ge(s_act, q + 1)
                nc.vector.tensor_tensor(U[:, p, :], U[:, p, :], G[:, p, :], ALU.mult).then_inc(s_prod, 1)
                dve.wait_ge(s_ahi, q + 1)
                nc.vector.tensor_tensor(a_lo[:, chunk, :], U[:, p, :], a_hi[:, chunk, :].bitcast(F32), ALU.subtract
                                        ).then_inc(s_a, 1)
                next_slot(n + 1, s + 1)

            def to_f(b, m, how, tok=slice(0, T)):
                if how == "set":
                    return nc.vector.tensor_copy(f[:, m, tok], bank[b][:, tok])
                if how == "add":
                    return nc.vector.tensor_tensor(f[:, m, tok], bank[b][:, tok], f[:, m, tok], ALU.add)
                return nc.vector.tensor_scalar(f[:, m, tok], bank[b][:, tok], col(how, m), None, ALU.add)

            def evacuate(n, s, m, how):
                dve.wait_ge(s_mm, n + 1)
                to_f(s, m, how).then_inc(s_evac, 1)

            def add_f_square(sub, m):
                dve.wait_ge(s_fsq, KD * sub + m + 1)
                if m > 1:
                    dve.wait_ge(s_facc, (KD - 2) * sub + m - 1)
                nc.vector.tensor_tensor(ss[:, :], ss[:, :], sq[:, m % 2, :], ALU.add).then_inc(s_facc, 1)

            def down(n0, how, last_of=None):
                if last_of is None:
                    with dve.Fori(0, KD // RING) as i:
                        for s in range(RING):
                            n = RING * i + (n0 + s)
                            next_slot(n, s)
                            evacuate(n, s, bass.ds(RING * i + s, 1), how)
                    return
                for m in range(KD):
                    n, s = n0 + m, m % RING
                    if m >= 2:
                        add_f_square(last_of, m - 1)
                    if m < KD - 1:
                        evacuate(n, s, m, how)
                    else:
                        dve.wait_ge(s_mm0, last_of + 1)
                        to_f(6, m, how, HALVES[0]).then_inc(s_evac0, 1)
                        if n + RING < SLOTS:
                            next_slot(n - 1, s - 1)
                        dve.wait_ge(s_mm, n + 1)
                        to_f(s, m, how, HALVES[1]).then_inc(s_evac, 1)
                    if n + RING < SLOTS and m < KD - 2:
                        next_slot(n, s)

            def boundary(sub, n0):
                invert(2 * sub + 2)
                if sub < SUBS - 1:
                    next_slot(n0 - 1, RING - 1)
                dve.wait_ge(s_bc, 2 * sub + 2)

                def normalise(k):
                    nc.vector.tensor_tensor(f[:, k, :], f[:, k, :], BCAST[:, :], ALU.mult).then_inc(s_dve, 1)
                    chain[0] += 1

                def add_residual(k):
                    dve.wait_ge(s_dve, chain[0])
                    nc.vector.scalar_tensor_tensor(out=h[:, k, :], in0=f[:, k, :], scalar=col("post", sub * KD + k),
                                                   in1=h[:, k, :], op0=ALU.mult, op1=ALU.add).then_inc(s_h, 1)

                if sub == SUBS - 1:
                    for k in range(PE_OUT):
                        nc.vector.tensor_tensor(f[:, k, :], f[:, k, :], BCAST[:, :], ALU.mult).then_inc(s_fn, 1)
                    for k in range(PE_OUT, KD, 2):
                        normalise(k)
                        normalise(k + 1)
                        add_residual(k)
                        add_residual(k + 1)
                    return
                for k in range(KD):
                    normalise(k)
                    if k:
                        x_lo_of(sub + 1, k - 1)
                    add_residual(k)
                    if k >= 2:
                        add_h_square(sub + 1, k - 1)
                x_lo_of(sub + 1, KD - 1)
                invert(2 * sub + 3)
                next_slot(n0, 0)

            def ffn(n0, index, sub):
                n, q = n0, KF * index
                for g, chunks in enumerate(FFN_GROUPS):
                    if g == 0:
                        for p in range(2):
                            pair_steps(n + 2 * p, 2 * p, q + p, p, sub + 1, first=(p == 0))
                    with dve.Fori(1 if g == 0 else 0, 2 * chunks // RING) as i:
                        for p in range(2):
                            pair_steps(RING * i + (n + 2 * p), 2 * p, 2 * i + (q + p), bass.ds(2 * i + p, 1),
                                       sub + 1)
                    n += 2 * chunks
                    down(n, "add" if g else "set", sub if g == len(FFN_GROUPS) - 1 else None)
                    n += KD
                    q += chunks
                boundary(sub, n0 + FFN_SLOTS)

            def qkv(n0):
                dve.wait_ge(s_const, CONSTS)

                def rotate(c):
                    x = kT[:, c, :] if c < 2 else qT[:, c - 2, :]
                    dve.wait_ge(s_perm, c + 1)
                    nc.vector.tensor_tensor(U[:, 0, :], bank[6 + c % 2][:, :], rs[:, :], ALU.mult)
                    link(nc.vector.tensor_tensor(U[:, 1, :], x, rc[:, :], ALU.mult))
                    nc.vector.tensor_tensor(x, U[:, 0, :], U[:, 1, :], ALU.add).then_inc(s_rope, 1)
                    dve.wait_ge(s_rope, c + 1)

                after = {4: (0, 1), 5: (2, 3), 6: (4, 5), 7: (6,), 8: (7,), 9: (8,), 10: (9,)}
                for c in range(QKV_SLOTS):
                    n, s = n0 + c, c % RING
                    if c == QKV_SLOTS - 1:
                        maxima(0)
                        maxima(1)
                        normalise(0)
                    elif c:
                        next_slot(n, s)
                    if c < 10:
                        if c >= 2:
                            dve.wait_ge(s_qb, c - 1)
                        scale_to(G[:, c % 2, :], s, n, 2)
                    for j in after.get(c, ()):
                        rotate(j)
                dve.wait_ge(s_mm, n0 + QKV_SLOTS)
                for t in range(NB):
                    nc.vector.scalar_tensor_tensor(out=V[:, t, :], in0=v_out(t),
                                                   scalar=r_col[:, t:t + 1],
                                                   in1=cols[:, COLS["b_v"]:COLS["b_v"] + 2 * P],
                                                   op0=ALU.mult, op1=ALU.add).then_inc(s_evac if t % 2 else s_v, 1)

            def maxima(t):
                n, cp = divmod(t, 4)
                i = t % 2
                sinks = cols[:, COLS["sinks"] + 4 * cp:COLS["sinks"] + 4 * cp + 4]
                dve.wait_ge(s_qk, t + 1)
                if t >= 2:
                    dve.wait_ge(s_exp, t - 1)
                for b in range(2):
                    ins = nc.vector.reduce_max(mx[:, i, 2 * b:2 * b + 2],
                                               scored(bank[(4, 0)[i] + b], n),
                                               axis=AX.X)
                link(ins)
                link(nc.vector.scalar_tensor_tensor(out=m_row[:, :], in0=mx[:, i, :], scalar=HD ** -0.5,
                                                    in1=sinks, op0=ALU.mult, op1=ALU.max))
                nc.vector.tensor_scalar(neg_m[:, i, :], m_row[:, :], -1.0, None, ALU.mult)
                nc.vector.tensor_tensor(sink_in[:, i, :], sinks, m_row[:, :], ALU.subtract).then_inc(s_m, 1)

            def normalise(t):
                i = t % 2
                dve.wait_ge(s_exp, t + 1)
                link(nc.vector.tensor_tensor(den[:, :], row_sum[:, i, :], sink_e[:, i, :], ALU.add))
                link(nc.vector.reciprocal(den[:, :], den[:, :]))
                for j in range(4):
                    at = slice(2 * P - keys(t // 4), 2 * P)
                    ins = nc.vector.tensor_scalar(prob[i][:, j, at], prob[i][:, j, at], den[:, j:j + 1], None,
                                                  ALU.mult)
                ins.then_inc(s_p, 1)

            def attention():
                def copy_own(t):
                    dve.wait_ge(s_t, t + 1)
                    if t >= 2:
                        dve.wait_ge(s_pv, t - 1)
                    nc.vector.tensor_copy(probT[t % 2][:, 1, :], bank[7][:, :]).then_inc(s_tb, 1)

                def out_lo(t):
                    n, cp = divmod(t, 4)
                    at = slice(2 * cp, 2 * cp + 2), slice(n * P, (n + 1) * P)
                    dve.wait_ge(s_ohi, t + 1)
                    nc.vector.tensor_tensor(a_lo[:, at[0], at[1]],
                                            bank[2 + t % 2][:, 0:2 * P].rearrange("p (c q) -> p c q", c=2),
                                            a_hi[:, at[0], at[1]].bitcast(F32), ALU.subtract).then_inc(s_o, 1)

                steps = 4 * NB
                for t in range(steps):
                    if t:
                        normalise(t)
                    if t + 2 < steps:
                        maxima(t + 2)
                    if t:
                        out_lo(t - 1)
                    copy_own(t)
                out_lo(steps - 1)
                next_slot(WO - 1, (WO - 1) % RING)

            def conv(n0):
                def gate(j):
                    if j >= 2:
                        dve.wait_ge(s_ud[j % 2], 16 * (j // 2))
                    dve.wait_ge(s_sig, j + 1)
                    nc.vector.scalar_tensor_tensor(out=u[j % 2].rearrange("p (q n) -> p n q", q=PH),
                                                   in0=U[:, j % 2, :].rearrange("p (n q) -> p n q", q=PH),
                                                   scalar=col("b_pw1", j),
                                                   in1=G[:, j % 2, :].rearrange("p (n q) -> p n q", q=PH),
                                                   op0=ALU.add, op1=ALU.mult).then_inc(s_u, 1)

                def matrices(j):
                    shape = [P, SHIFTS, GC, PH]
                    dve.wait_ge(s_taps[j % 2], 16 * (j // 2 + 1))
                    for g in range(GROUPS):
                        if j:
                            dve.wait_ge(s_cv, GROUPS * (j - 1) + g + 1)
                        nc.vector.tensor_tensor(mats[g], same_c[:, None, :, None].broadcast_to(shape),
                                                taps[:, j % 2, g, :, None, :].broadcast_to(shape), ALU.mult
                                                ).then_inc(s_mat, 1)

                def biased(j):
                    dve.wait_ge(s_cv, GROUPS * (j + 1))
                    if j >= 4:
                        dve.wait_ge(s_zd[j % 4], 16)
                        dve.wait_ge(s_zsq, j - 3)
                    if j - 4 >= EARLY:
                        dve.wait_ge(s_dlmm, j - 4 - EARLY + 1)
                    nc.vector.tensor_tensor(zg[j % 4], bank[6 + j % 2][:, :].rearrange("p (g n) -> p g n", g=GROUPS),
                                            b_dw[:, GROUPS * j:GROUPS * (j + 1), None].broadcast_to([P, GROUPS, NT]),
                                            ALU.add).then_inc(s_zg, 1)

                def centre(j):
                    dve.wait_ge(s_zg, j + 1)
                    nc.vector.tensor_tensor(zg[j % 4], zg[j % 4], m0[:, None, :].broadcast_to([P, GROUPS, NT]),
                                            ALU.subtract).then_inc(s_zc, 1)

                def on_phases(out, v, done):
                    nc.vector.tensor_tensor(out.rearrange("p (q n) -> p q n", q=PH),
                                            ident[:, 0:PH, None].broadcast_to([P, PH, NT]),
                                            v[:, None, :].broadcast_to([P, PH, NT]), ALU.mult).then_inc(done, 1)

                for j in range(KD):
                    for e in range(2):
                        n = n0 + 2 * j + e
                        if n > n0:
                            next_slot(n, n % RING)
                        scale_to((U, G)[e][:, j % 2, :], n % RING, n, 5)
                        if (j, e) == (KD - 1, 0):
                            matrices(6)
                            biased(5)
                            centre(5)
                    gate(j)
                    if 1 <= j < KD - 2:
                        matrices(j - 1)
                    if 2 <= j < KD - 2:
                        biased(j - 2)
                        dve.wait_ge(s_zg, j - 1)
                        nc.vector.reduce_sum(early[:, j - 2, :], zg[j - 2].rearrange("p g n -> p n g"), axis=AX.X
                                             ).then_inc(s_early, 1)
                    if j == KD - 2:
                        dve.wait_ge(s_m0mm, 1)
                        nc.vector.tensor_scalar(m0[:, :], BCAST[:, 0:NT], 1.0 / (EARLY * P), None, ALU.mult
                                                ).then_inc(s_m0, 1)
                        dve.wait_ge(s_m0, 1)
                        for i in range(EARLY):
                            centre(i)
                        matrices(5)
                        biased(4)
                        centre(4)
                matrices(7)
                for i in (6, 7):
                    biased(i)
                    centre(i)
                dve.wait_ge(s_dlmm, KD - EARLY)
                nc.vector.tensor_scalar(dl[:, :], BCAST[:, 0:NT], 1.0 / D, None, ALU.mult).then_inc(s_dl, 1)
                dve.wait_ge(s_dl, 1)
                on_phases(dl_diag, dl, s_dldiag)
                link(nc.vector.tensor_tensor(dl_sq[:, :], dl[:, :], dl[:, :], ALU.mult))
                dve.wait_ge(s_sqmm, KD)
                link(nc.vector.scalar_tensor_tensor(out=var[:, :], in0=STAT[:, 0:NT], scalar=1.0 / D, in1=dl_sq[:, :],
                                                    op0=ALU.mult, op1=ALU.subtract))
                nc.vector.tensor_scalar(var[:, :], var[:, :], 0.0, None, ALU.max).then_inc(s_var, 1)
                dve.wait_ge(s_lroot, 1)
                link(nc.vector.reciprocal(std[:, :], std[:, :]))
                on_phases(std_diag, std, s_ldiag)
                for m in range(KD):
                    dve.wait_ge(s_y[m], 16)
                    if m == 0:
                        dve.wait_ge(s_lbc, 1)
                    link(nc.vector.tensor_tensor(y[:, m, :], y[:, m, :], bank[6][:, :], ALU.subtract))
                    if m == 0:
                        dve.wait_ge(s_lbc, 2)
                    nc.vector.tensor_tensor(y[:, m, :], y[:, m, :], bank[7][:, :], ALU.mult).then_inc(s_z, 1)
                    if m:
                        z_lo_of(m - 1)
                z_lo_of(KD - 1)

            def z_lo_of(m):
                dve.wait_ge(s_zhi, m + 1)
                nc.vector.tensor_tensor(a_lo[:, m, :], f[:, m, :], a_hi[:, m, :].bitcast(F32), ALU.subtract
                                        ).then_inc(s_zlo, 1)

            nc.vector.memset(eps[:, 0:1], EPS)
            nc.vector.memset(eps[:, 1:2], LN_EPS)
            nc.vector.memset(ones[:, :], 1.0).then_inc(s_ones, 1)
            dve.wait_ge(s_cols, 16)
            for sub in HALF_WEIGHT:
                at = cols[:, COLS["post"] + sub * KD:COLS["post"] + (sub + 1) * KD]
                ins = nc.vector.tensor_scalar(at, at, 0.5, None, ALU.mult)
            ins.then_inc(s_half, 1)
            dve.wait_ge(s_half, 1)
            for k in range(KD):
                x_lo_of(0, k)
                if k in (0, 2):
                    at = slice(k // 2 * SLOT // 2, (k // 2 + 1) * SLOT // 2)
                    for s in range(RING):
                        dve.wait_ge((s_hi0, s_hi)[k // 2], s + 1)
                        nc.vector.tensor_tensor(w_lo[:, s, at], raw[:, s, at], w_hi[:, s, at].bitcast(F32),
                                                ALU.subtract).then_inc((s_lo0, s_lo)[k // 2], 1)
                if 1 <= k <= KD - 2:
                    add_h_square(0, k)
            dve.wait_ge(s_const, CONSTS)
            invert(1)
            next_slot(0, 0)
            ffn(FFN0, 0, 0)
            qkv(QKV)
            attention()
            down(WO, "b_o", 1)
            boundary(1, FFN1)
            ffn(FFN1, 1, 2)
            ffn(FFN2, 2, 3)
            conv(PW1)
            down(PW2, "b_pw2", 4)
            boundary(4, FFN3)
            ffn(FFN3, 3, 5)


def up_slots(w):
    n = w.shape[1] // P
    return w.reshape(KD, P, n, P).transpose(2, 1, 0, 3).reshape(n, P, SLOT)


def down_slots(w):
    k = w.shape[0] // P
    out = np.zeros((KD, P, BLK, P), w.dtype)
    out[:, :, :k] = w.reshape(k, P, KD, P).transpose(2, 1, 0, 3)
    return out.reshape(KD, P, SLOT)


def ffn_slots(w_in, w_out):
    pairs = np.stack([up_slots(w_in[:, :FF]), up_slots(w_in[:, FF:])], 1)
    parts, c = [], 0
    for chunks in FFN_GROUPS:
        parts.append(pairs[c:c + chunks].reshape(2 * chunks, P, SLOT))
        parts.append(down_slots(w_out[c * P:(c + chunks) * P]))
        c += chunks
    return parts


def tables():
    pos = np.arange(T, dtype=np.float32)
    inv = np.float32(THETA) ** (-np.arange(0, ROT, 2, dtype=np.float32) / np.float32(ROT))
    ang = pos[None, :] * inv.astype(np.float32)[:, None]
    rc, rs = np.ones((P, T), np.float32), np.zeros((P, T), np.float32)
    perm = np.zeros((P, P), np.float32)
    r = ROT // 2
    for o in range(0, P, HD):
        rc[o:o + r] = rc[o + r:o + ROT] = np.cos(ang)
        rs[o:o + r], rs[o + r:o + ROT] = -np.sin(ang), np.sin(ang)
        for i in range(r):
            perm[o + i, o + r + i] = perm[o + r + i, o + i] = 1.0
    q, k = np.arange(P)[:, None], np.arange(2 * P)[None, :]
    diff = q + P - k
    band = (diff >= 0) & (diff < P)
    mask = np.repeat(np.where(band, 0.0, -1e30).astype(np.float32)[:, None], 2, 1)
    return rc, rs, perm, np.eye(P, dtype=np.float32), mask


def tap_places(w):
    out = np.zeros((KD, GC, PH, GROUPS, SHIFTS, PH), w.dtype)
    w = w.reshape(CW, KD, GROUPS, GC)
    for m in range(SHIFTS):
        for p in range(PH):
            for q in range(PH):
                tap = CW - 1 + PH * (m - PAD) + p - q
                if 0 <= tap < CW:
                    out[:, :, p, :, m, q] = w[tap].transpose(0, 2, 1)
    return out.reshape(KD, P, GROUPS * TAPS)


def group_tables():
    i = np.arange(P)
    same_c = (i[:, None] // PH == np.arange(GC)[None, :]).astype(np.float32)
    same_q = (i[:, None] % PH == i[None, :] % PH).astype(np.float32)
    return same_c, same_q


def kernel(x, norm_pre, norm_post, w_ffn_in, w_ffn_out, attn_w_qkv, attn_b_qkv, attn_w_o, attn_b_o, attn_sinks,
           conv_w_pw1, conv_b_pw1, conv_w_dw, conv_b_dw, conv_ln_g, conv_ln_b, conv_w_pw2, conv_b_pw2):
    import concourse.bacc as bacc
    import ml_dtypes
    from concourse.bass_utils import run_bass_kernel_spmd

    given = dict(locals())
    (x, norm_pre, norm_post, w_ffn_in, w_ffn_out, w_qkv, b_qkv, w_o, b_o, sinks, w_pw1, b_pw1, w_dw, b_dw, ln_g, ln_b,
     w_pw2, b_pw2) = (np.asarray(given[n]) for n in kernel.__code__.co_varnames[:kernel.__code__.co_argcount])

    heads = [head_of(c // 2, b, c % 2) for c in range(KD) for b in range(2)]
    q_cols = np.concatenate([np.arange(hd * HD, (hd + 1) * HD) for hd in heads])
    q_dim, kv_dim = HEADS * HD, KV * HD
    qk_cols = np.concatenate([q_dim + np.arange(kv_dim), q_cols])
    w_v = w_qkv[0][:, q_dim + kv_dim:].reshape(2, 4, P, kv_dim).transpose(0, 2, 1, 3).reshape(2, P, SLOT)
    pw1 = np.stack([up_slots(w_pw1[0][:, :D]), up_slots(w_pw1[0][:, D:])], 1).reshape(2 * KD, P, SLOT)
    stream = np.concatenate(
        ffn_slots(w_ffn_in[0, 0], w_ffn_out[0, 0])
        + [up_slots(w_qkv[0][:, qk_cols]), w_v, down_slots(w_o[0][q_cols])]
        + ffn_slots(w_ffn_in[0, 1], w_ffn_out[0, 1]) + ffn_slots(w_ffn_in[1, 0], w_ffn_out[1, 0])
        + [pw1, down_slots(w_pw2[0])] + ffn_slots(w_ffn_in[1, 1], w_ffn_out[1, 1]))

    def cols(v):
        return v.reshape(-1, P).T

    sink_order = [head_of(cp, b, cc) for cp in range(4) for b in range(2) for cc in range(2)]
    col_in = np.concatenate(
        [cols(norm_pre), cols(norm_post), cols(b_qkv[0][qk_cols]), cols(b_o), cols(b_pw1), cols(ln_g), cols(ln_b),
         cols(b_pw2),
         np.broadcast_to(sinks[0][sink_order], (P, HEADS)), np.broadcast_to(b_qkv[0][q_dim + kv_dim:], (P, kv_dim))], 1)
    rc, rs, perm, ident, mask = tables()
    same_c, same_q = group_tables()
    b_groups = np.broadcast_to(b_dw.reshape(KD * GROUPS, GC, 1), (KD * GROUPS, GC, PH)).reshape(KD * GROUPS, P).T
    bf = ml_dtypes.bfloat16
    ins = {"stream": stream, "xT": np.ascontiguousarray(x[0].T), "cols_in": np.ascontiguousarray(col_in),
           "rope_c": rc, "rope_s": rs, "perm_in": perm, "ident_in": ident, "ident_b_in": ident.astype(bf),
           "mask_in": mask.astype(bf), "taps_in": tap_places(w_dw.reshape(CW, D)),
           "conv_in": np.concatenate([same_c, same_q, b_groups], 1)}

    nc = bacc.Bacc("TRN2", target_bir_lowering=False, num_devices=1)
    args = [nc.dram_tensor(n, a.shape, mybir.dt.from_np(a.dtype), kind="ExternalInput").ap() for n, a in ins.items()]
    out = nc.dram_tensor("outT", (D, T), F32, kind="ExternalOutput").ap()
    scratch = [nc.dram_tensor(n, (KD, P, T), F32).ap() for n in ("u_scratch", "z_scratch")]
    build_program(nc, *args, *scratch, out)
    r = run_bass_kernel_spmd(nc, [ins], core_ids=[0])
    return np.ascontiguousarray(r.results[0]["outT"].T)[None]
```
